# Optimizing a Trainium2 kernel written in Bass

```python
import jax, jax.numpy as jnp
from jax import lax
import numpy as np

D_MODEL = 1024
BATCH = 1
SEQ = 512
DEPTH = 1
DEC_BATCH = 8
DEC_SEQ = 4
PAST_LEN = 2048
PAGE_SIZE = 128

HEAD_DIM = 64
N_Q_HEADS = 16
N_KV_HEADS = 2
GQA_GROUP = N_Q_HEADS // N_KV_HEADS
WINDOW = 128
ROPE_THETA = 10000.0
POOL_WIDTH = D_MODEL
POOL_WINDOWS = (2, 4, 8, 16)
N_POOL_GROUPS = len(POOL_WINDOWS)
POOL_GROUP_WIDTH = POOL_WIDTH // N_POOL_GROUPS
POOL_STATE_LEN = max(POOL_WINDOWS) - 1
N_EXPERT_GROUPS = 4
EXPERTS_PER_GROUP = 8
N_EXPERTS = N_EXPERT_GROUPS * EXPERTS_PER_GROUP
TOP_K_INNER = 2
D_EXPERT = 512
MOE_BLOCK = 128
RMS_EPS = 1e-6
Q_W = N_Q_HEADS * HEAD_DIM
KV_W = N_KV_HEADS * HEAD_DIM
OFF_K = Q_W
OFF_V = OFF_K + KV_W
OFF_U = OFF_V + KV_W
OFF_GA = OFF_U + POOL_WIDTH
OFF_GP = OFF_GA + D_MODEL
IN_W = OFF_GP + D_MODEL

kernel_name = 'hybrid_swa_sink_pool_hmoe_step'

def rms_norm(x, g):
    xf = x.astype(jnp.float32)
    y = xf * lax.rsqrt(jnp.mean(xf * xf, axis=-1, keepdims=True) + RMS_EPS)
    return (y * g.astype(jnp.float32)).astype(x.dtype)

def rope(x, pos):
    half = HEAD_DIM // 2
    inv = ROPE_THETA ** (-jnp.arange(half, dtype=jnp.float32) * (2.0 / HEAD_DIM))
    ang = pos.astype(jnp.float32)[:, None] * inv[None, :]
    cos = jnp.cos(ang)[None, :, None, :]
    sin = jnp.sin(ang)[None, :, None, :]
    xf = x.astype(jnp.float32)
    x1, x2 = xf[..., :half], xf[..., half:]
    return jnp.concatenate([x1 * cos - x2 * sin, x2 * cos + x1 * sin], axis=-1).astype(x.dtype)

def sink_window_attention(q, k, v, q_pos, k_pos, sinks):
    s = jnp.einsum('bnqhgd,bnkhd->bnhgqk', q.astype(jnp.float32), k.astype(jnp.float32)) * (HEAD_DIM ** -0.5)
    rel = q_pos[:, :, None] - k_pos[:, None, :]
    mask = (rel >= 0) & (rel < WINDOW) & (k_pos[:, None, :] >= 0)
    s = jnp.where(mask[None, :, None, None], s, -jnp.inf)
    sink = sinks.astype(jnp.float32).reshape(N_KV_HEADS, GQA_GROUP)[None, None, :, :, None, None]
    m = jnp.maximum(jnp.max(s, axis=-1, keepdims=True), sink)
    p = jnp.exp(s - m)
    denom = jnp.sum(p, axis=-1, keepdims=True) + jnp.exp(sink - m)
    return jnp.einsum('bnhgqk,bnkhd->bnqhgd', p / denom, v.astype(jnp.float32))

def multiscale_pool(ext, first_pos, n_out):
    B, R, _ = ext.shape
    e = ext.astype(jnp.float32).reshape(B, R, N_POOL_GROUPS, POOL_GROUP_WIDTH)
    csum = jnp.concatenate([jnp.zeros_like(e[:, :1]), jnp.cumsum(e, axis=1)], axis=1)
    rows = jnp.arange(R - n_out, R, dtype=jnp.int32)
    pos = first_pos + rows
    means = []
    for g, w in enumerate(POOL_WINDOWS):
        lo = jnp.maximum(rows + 1 - w, 0)
        c = csum[:, :, g]
        window_sum = c[:, R - n_out + 1:] - jnp.take(c, lo, axis=1)
        count = jnp.minimum(w, pos + 1).astype(jnp.float32)
        means.append(window_sum / count[None, :, None])
    return jnp.stack(means, axis=2) - e[:, R - n_out:]

def hier_moe(h, w_route_group, b_route_group, w_route_expert, b_route_expert, w_gate, w_up, w_down):
    N, D = h.shape
    hf = h.astype(jnp.float32)
    g_prob = jax.nn.softmax(hf @ w_route_group.astype(jnp.float32) + b_route_group.astype(jnp.float32), axis=-1)
    g_w, g_idx = lax.top_k(g_prob, 1)
    e_logits = (hf @ w_route_expert.astype(jnp.float32) + b_route_expert.astype(jnp.float32)).reshape(N, N_EXPERT_GROUPS, EXPERTS_PER_GROUP)
    e_logits = e_logits[jnp.arange(N), g_idx[:, 0]]
    top_l, top_i = lax.top_k(e_logits, TOP_K_INNER)
    comb = g_w * jax.nn.softmax(top_l, axis=-1)
    eid = g_idx * EXPERTS_PER_GROUP + top_i
    A = N * TOP_K_INNER
    flat_e = eid.reshape(A)
    flat_tok = jnp.arange(A, dtype=jnp.int32) // TOP_K_INNER
    flat_w = comb.reshape(A)
    order = jnp.argsort(flat_e)
    se, stok, sw = flat_e[order], flat_tok[order], flat_w[order]
    counts = jnp.bincount(flat_e, length=N_EXPERTS)
    starts = jnp.cumsum(counts) - counts
    pcounts = (counts + MOE_BLOCK - 1) // MOE_BLOCK * MOE_BLOCK
    pends = jnp.cumsum(pcounts)
    pstarts = pends - pcounts
    dest = pstarts[se] + jnp.arange(A, dtype=jnp.int32) - starts[se]
    n_blocks = -(-(A + N_EXPERTS * (MOE_BLOCK - 1)) // MOE_BLOCK)
    xp = jnp.zeros((n_blocks * MOE_BLOCK, D), h.dtype).at[dest].set(h[stok])
    block_e = jnp.minimum(jnp.searchsorted(pends, jnp.arange(n_blocks, dtype=jnp.int32) * MOE_BLOCK, side='right'), N_EXPERTS - 1)

    def expert_block(args):
        xb, e = args
        return (jax.nn.silu(xb @ w_gate[e]) * (xb @ w_up[e])) @ w_down[e]

    yp = lax.map(expert_block, (xp.reshape(n_blocks, MOE_BLOCK, D), block_e)).reshape(n_blocks * MOE_BLOCK, D)
    out = jnp.zeros((N, D), jnp.float32).at[stok].add(yp[dest].astype(jnp.float32) * sw[:, None])
    return out.astype(h.dtype)

def decoder_layer(x, start, past_k, past_v, past_u, w):
    B, S, _ = x.shape
    pos = start + jnp.arange(S, dtype=jnp.int32)
    h = rms_norm(x, w['norm_mix_g'])
    z = h @ w['w_in']
    q = z[..., :OFF_K].reshape(B, S, N_Q_HEADS, HEAD_DIM)
    k = z[..., OFF_K:OFF_V].reshape(B, S, N_KV_HEADS, HEAD_DIM)
    v = z[..., OFF_V:OFF_U].reshape(B, S, N_KV_HEADS, HEAD_DIM)
    u = z[..., OFF_U:OFF_GA]
    ga = z[..., OFF_GA:OFF_GP]
    gp = z[..., OFF_GP:]
    q = rope(rms_norm(q, w['q_norm_g']), pos)
    k = rope(rms_norm(k, w['k_norm_g']), pos)
    if past_k is None:
        nb = S // WINDOW
        qb = q.reshape(B, nb, WINDOW, N_KV_HEADS, GQA_GROUP, HEAD_DIM)
        kb = k.reshape(B, nb, WINDOW, N_KV_HEADS, HEAD_DIM)
        vb = v.reshape(B, nb, WINDOW, N_KV_HEADS, HEAD_DIM)
        shift = lambda t: jnp.concatenate([jnp.zeros_like(t[:, :1]), t[:, :-1]], axis=1)
        k_band = jnp.concatenate([shift(kb), kb], axis=2)
        v_band = jnp.concatenate([shift(vb), vb], axis=2)
        q_pos = pos.reshape(nb, WINDOW)
        k_pos = jnp.concatenate([q_pos - WINDOW, q_pos], axis=1)
        new_k, new_v = k[:, -WINDOW:], v[:, -WINDOW:]
        ext, first = u, start
        new_u = u[:, -POOL_STATE_LEN:]
    else:
        k_all = jnp.concatenate([past_k.astype(k.dtype), k], axis=1)
        v_all = jnp.concatenate([past_v.astype(v.dtype), v], axis=1)
        qb = q.reshape(B, 1, S, N_KV_HEADS, GQA_GROUP, HEAD_DIM)
        k_band, v_band = k_all[:, None], v_all[:, None]
        q_pos = pos[None]
        k_pos = jnp.concatenate([start - WINDOW + jnp.arange(WINDOW, dtype=jnp.int32), pos])[None]
        new_k, new_v = k_all[:, -WINDOW:], v_all[:, -WINDOW:]
        ext = jnp.concatenate([past_u.astype(u.dtype), u], axis=1)
        first = start - POOL_STATE_LEN
        new_u = ext[:, -POOL_STATE_LEN:]
    attn = sink_window_attention(qb, k_band, v_band, q_pos, k_pos, w['attn_sinks']).reshape(B, S, Q_W).astype(x.dtype)
    pooled = multiscale_pool(ext, first, S)
    pooled = jnp.einsum('bsgc,gcd->bsgd', pooled, w['pool_mix_w'].astype(jnp.float32)).reshape(B, S, POOL_WIDTH)
    pooled = (pooled * w['pool_scale'].astype(jnp.float32)).astype(x.dtype)
    merged = jax.nn.sigmoid(ga) * (attn @ w['w_attn_branch']) + jax.nn.sigmoid(gp) * (pooled @ w['w_pool_branch'])
    x = x + merged @ w['w_out']
    hn = rms_norm(x, w['norm_ffn_g']).reshape(B * S, D_MODEL)
    x = x + hier_moe(hn, w['w_route_group'], w['b_route_group'], w['w_route_expert'], w['b_route_expert'],
                     w['w_expert_gate'], w['w_expert_up'], w['w_expert_down']).reshape(B, S, D_MODEL)
    return x, new_k, new_v, new_u

def setup_inputs(seed: int = 0) -> dict:
    key = jax.random.key(seed)
    ks = jax.random.split(key, 24)
    L = DEPTH
    C = POOL_GROUP_WIDTH
    nrm = lambda k, shape, scale: jax.random.normal(k, shape, jnp.float32) * scale
    return {
        'x_prompt': nrm(ks[0], (BATCH, SEQ, D_MODEL), 1.0),
        'x_sample': nrm(ks[1], (DEC_BATCH, DEC_SEQ, D_MODEL), 1.0),
        'cache_k': nrm(ks[2], (L, DEC_BATCH, WINDOW, N_KV_HEADS, HEAD_DIM), 1.0),
        'cache_v': nrm(ks[3], (L, DEC_BATCH, WINDOW, N_KV_HEADS, HEAD_DIM), 1.0),
        'state_pool': nrm(ks[4], (L, DEC_BATCH, POOL_STATE_LEN, POOL_WIDTH), 1.0),
        'norm_mix_g': 1.0 + nrm(ks[5], (L, D_MODEL), 0.05),
        'w_in': nrm(ks[6], (L, D_MODEL, IN_W), D_MODEL ** -0.5),
        'q_norm_g': 1.0 + nrm(ks[7], (L, HEAD_DIM), 0.05),
        'k_norm_g': 1.0 + nrm(ks[8], (L, HEAD_DIM), 0.05),
        'attn_sinks': nrm(ks[9], (L, N_Q_HEADS), 1.0),
        'w_attn_branch': nrm(ks[10], (L, Q_W, D_MODEL), Q_W ** -0.5),
        'pool_mix_w': nrm(ks[11], (L, N_POOL_GROUPS, C, C), C ** -0.5),
        'pool_scale': 1.0 + nrm(ks[12], (L, POOL_WIDTH), 0.1),
        'w_pool_branch': nrm(ks[13], (L, POOL_WIDTH, D_MODEL), POOL_WIDTH ** -0.5),
        'w_out': nrm(ks[14], (L, D_MODEL, D_MODEL), D_MODEL ** -0.5),
        'norm_ffn_g': 1.0 + nrm(ks[15], (L, D_MODEL), 0.05),
        'w_route_group': nrm(ks[16], (L, D_MODEL, N_EXPERT_GROUPS), D_MODEL ** -0.5),
        'b_route_group': nrm(ks[17], (L, N_EXPERT_GROUPS), 0.01),
        'w_route_expert': nrm(ks[18], (L, D_MODEL, N_EXPERTS), D_MODEL ** -0.5),
        'b_route_expert': nrm(ks[19], (L, N_EXPERTS), 0.01),
        'w_expert_gate': nrm(ks[20], (L, N_EXPERTS, D_MODEL, D_EXPERT), D_MODEL ** -0.5),
        'w_expert_up': nrm(ks[21], (L, N_EXPERTS, D_MODEL, D_EXPERT), D_MODEL ** -0.5),
        'w_expert_down': nrm(ks[22], (L, N_EXPERTS, D_EXPERT, D_MODEL), D_EXPERT ** -0.5),
    }

def reference(x_prompt, x_sample, cache_k, cache_v, state_pool, norm_mix_g, w_in, q_norm_g, k_norm_g,
              attn_sinks, w_attn_branch, pool_mix_w, pool_scale, w_pool_branch, w_out, norm_ffn_g,
              w_route_group, b_route_group, w_route_expert, b_route_expert, w_expert_gate, w_expert_up,
              w_expert_down):
    xp, xs = x_prompt, x_sample
    kp, vp, up, ksl, vsl, usl = [], [], [], [], [], []
    for l in range(DEPTH):
        w = dict(norm_mix_g=norm_mix_g[l], w_in=w_in[l], q_norm_g=q_norm_g[l], k_norm_g=k_norm_g[l],
                 attn_sinks=attn_sinks[l], w_attn_branch=w_attn_branch[l], pool_mix_w=pool_mix_w[l],
                 pool_scale=pool_scale[l], w_pool_branch=w_pool_branch[l], w_out=w_out[l],
                 norm_ffn_g=norm_ffn_g[l], w_route_group=w_route_group[l], b_route_group=b_route_group[l],
                 w_route_expert=w_route_expert[l], b_route_expert=b_route_expert[l],
                 w_expert_gate=w_expert_gate[l], w_expert_up=w_expert_up[l], w_expert_down=w_expert_down[l])
        xp, nk, nv, nu = decoder_layer(xp, 0, None, None, None, w)
        kp.append(nk); vp.append(nv); up.append(nu)
        xs, nk, nv, nu = decoder_layer(xs, PAST_LEN, cache_k[l], cache_v[l], state_pool[l], w)
        ksl.append(nk); vsl.append(nv); usl.append(nu)
    return (xp, xs, jnp.stack(kp), jnp.stack(vp), jnp.stack(up), jnp.stack(ksl), jnp.stack(vsl), jnp.stack(usl))


_drawn_inputs = setup_inputs


def setup_inputs(seed=0):
    import zlib

    import numpy as np

    out = dict(_drawn_inputs(seed))
    spreads = {}
    factors = {'q_norm_g': 3.873, 'attn_sinks': 4.606, 'b_route_group': 6.363, 'b_route_expert': 5.149}
    for name, (base, spread) in spreads.items():
        noise = np.random.default_rng([zlib.crc32(name.encode()), seed]).standard_normal(out[name].shape)
        drawn = base * np.exp(spread * noise) if base else spread * noise
        out[name] = __import__('jax').numpy.asarray(drawn.astype(out[name].dtype))
    for name, factor in factors.items():
        out[name] = (out[name] * factor).astype(out[name].dtype)
    return out
```

```python
from contextlib import ExitStack

import numpy as np

import concourse.bass as bass
from concourse import mybir

ALU = mybir.AluOpType
ACT = mybir.ActivationFunctionType
AX_X = mybir.AxisListType.X
F32 = mybir.dt.float32
BF16 = mybir.dt.bfloat16
U32 = mybir.dt.uint32
I32 = mybir.dt.int32

P = 128
D = 1024
KD = D // P
SEQ = 512
DEC_B, DEC_S = 8, 4
DEC = DEC_B * DEC_S
T = SEQ + DEC
NT = 5
ROWS = [P, P, P, P, DEC]
HALF = T // 2
PAST_LEN = 2048
HD = 64
NKV, NI = 2, 8
NH = NKV * NI
WIN = 128
POOL_W = (2, 4, 8, 16)
PAST_U = 15
KV_OFF, U_OFF, GA_OFF, GP_OFF = 1024, 1280, 2304, 3328
EPS = 1e-6
NG, EG = 4, 8
NE = NG * EG
DE = 512
JX, JH = D // P, DE // P
C = 64
ROWS_SORTED = 2 * T
NOV = (ROWS_SORTED - 1) // C
XW = D + 8
NSLOT = 2
UNROLL = 2
BIG = 4096.0
MASKED = -1.0e30

UP = 16
USEG = UP + DEC_S
UW = UP + SEQ + DEC_B * USEG

CONST = {}
_at = 0
for _name, _n in (("ident", 128), ("dec_mask", 4 * 160), ("cos", NT * 32), ("sin", NT * 32),
                  ("inv_count", 4 * 16), ("live", NT), ("group_rank", NG), ("expert_rank", EG),
                  ("expert_id", NE), ("row", 1), ("chunk_edge", 8), ("item", NOV), ("before", P), ("band", 2 * P)):
    CONST[_name] = (_at, _n)
    _at += _n
NCONST = _at


def constants():
    c = np.zeros((P, NCONST), np.float32)

    def put(name, value):
        a, n = CONST[name]
        c[:, a:a + n] = np.asarray(value, np.float32).reshape(-1, n)

    put("ident", np.eye(P))
    m = np.full((P, 4, 160), MASKED, np.float32)
    for row in range(P):
        bb, s = row // 64, row % DEC_S
        for g in range(4):
            m[row, g, s + 1:128] = 0
            first = 128 + (2 * g + bb) * DEC_S
            m[row, g, first:first + s + 1] = 0
    put("dec_mask", m.reshape(P, -1))
    pos = np.zeros((P, NT), np.float32)
    for t in range(4):
        pos[:, t] = t * P + np.arange(P)
    pos[:, 4] = PAST_LEN + np.arange(P) % DEC_S
    inv = (np.float32(10000.0) ** (-np.arange(32, dtype=np.float32) * np.float32(2.0 / HD))).astype(np.float32)
    ang = pos[:, :, None] * inv[None, None, :]
    put("cos", np.cos(ang).reshape(P, -1))
    put("sin", np.sin(ang).reshape(P, -1))
    put("inv_count", np.array([[1.0 / min(w, t + 1) for t in range(16)] for w in POOL_W]).reshape(1, -1))
    live = np.ones((P, NT), np.float32)
    live[DEC:, 4] = 0
    put("live", live)
    put("group_rank", NG - np.arange(NG))
    put("expert_rank", EG - np.arange(EG))
    put("expert_id", np.arange(NE))
    put("row", np.arange(P).reshape(P, 1))
    put("chunk_edge", C * (1 + np.arange(8)))
    put("item", np.arange(NOV))
    q, k = np.arange(P)[:, None], np.arange(P)[None, :]
    put("before", q < k)
    put("band", np.concatenate([np.where(k > q, 0, MASKED), np.where(k <= q, 0, MASKED)], axis=1))
    return c


def above(eng, sem, value):
    if isinstance(value, int) and value <= 0:
        return
    eng.wait_ge(sem, value)


def build(nc, a, o):
    with ExitStack() as ctx:
        def sb(name, shape, dt=F32):
            return ctx.enter_context(nc.sbuf_tensor(name, shape, dt))

        def sem(name):
            return ctx.enter_context(nc.semaphore(name))

        x = sb("x", [P, NT, D])
        const = sb("const", [P, NCONST])
        cbf = sb("cbf", [P, 3 * P + NKV * 2 * P], BF16)
        g_mix = sb("g_mix", [P, KD])
        p_scale = sb("p_scale", [P, KD])
        sinks = sb("sinks", [P, NKV, NI])
        neg_sink = sb("neg_sink", [P, NI, NKV])
        dec_sink = sb("dec_sink", [P, 2])
        eps = sb("eps", [P, 1])
        r_bias = sb("r_bias", [P, NG + NE])
        w_route = sb("w_route", [P, KD, NG + NE])
        stat = sb("stat", [P, 3, NT])
        z_stat = sb("z_stat", [P, 2, 3, 8])
        a_stat = sb("a_stat", [P, 2, 4, 8])
        d_stat = sb("d_stat", [P, 4, 4])
        kT_pad = sb("kT_pad", [P, NKV, T])
        ARENA = 43648
        arena = sb("arena", [P, ARENA])

        def split(v, shape):
            if len(shape) == 1:
                return v
            names = "abcd"[:len(shape)]
            return v.rearrange(f"p ({' '.join(names)}) -> p {' '.join(names)}", **dict(zip(names, shape)))

        def area(at, *shape):
            n = int(np.prod(shape))
            assert at + n <= ARENA
            return split(arena[:, at:at + n], shape)

        hT = area(0, KD, T)
        attnT = area(4352, KD, T)
        mixedT = area(8704, KD, T)
        w_slot = [13056, 17152]
        pooledT = area(21248, KD, T)
        uT = area(25600, KD, UW)
        qT = area(31104, KD, T)
        mergedT = qT
        WORK = 35456
        xs = [area(31104 + s * D, D) for s in range(2)]
        x_sq = area(31104 + 2 * D, D)
        z_raw = [area(WORK + s * 512, 512) for s in range(2)]
        z_sq = [area(WORK + 1024 + s * 512, 512) for s in range(2)]
        z_norm, z_cos, z_sin = (area(WORK + 2048 + s * 512, 512) for s in range(3))
        q_rows = [area(WORK + 3584 + s * 512, 512) for s in range(2)]
        rot = area(4352, 4, NT, HD)
        g_qk = area(4352 + 4 * NT * HD, 2, HD)
        win_sum = [area(5760 + s * 2 * UW, 2, UW) for s in range(2)]
        kc_rows = area(8704, DEC_B, P)
        vc_rows = area(8704 + 1024, DEC_B, P)
        kcT_pad = area(8704 + 2048, DEC_B, NKV, P)
        past_u = area(21248, D)
        probs = [area(WORK + s * 2048, 2048) for s in range(2)]
        probsT = [area(WORK + 4096 + s * 512, 512) for s in range(4)]
        k_rows = area(WORK + 6144, NT, P)
        v_rows = area(WORK + 6784, NT, P)
        q_decT = area(WORK + 7424, DEC_B, NI, DEC_S)
        u_decT = area(WORK + 7680, KD, DEC)
        d_probs = area(WORK, 4, 256)
        new_u = area(WORK + 2048, 2, D)
        gates = [[area(25600 + (2 * h + j) * HALF, HALF) for j in range(2)] for h in range(2)]
        gated = [[area(25600 + (4 + 2 * h + j) * HALF, HALF) for j in range(2)] for h in range(2)]
        w_out = area(WORK, KD, D)
        hn = area(25600, NT, XW)
        hnT = [area(20480 + s * D, KD, P) for s in range(2)]
        R = 22528
        g_ffn = area(24576, D)
        w_up = [area(s * 12288, JX, DE) for s in range(NSLOT)]
        w_gate = [area(s * 12288 + 4096, JX, DE) for s in range(NSLOT)]
        w_down = [area(s * 12288 + 8192, JH, D) for s in range(NSLOT)]
        EW = 31104
        x_rows = [area(EW + s * XW, XW) for s in range(2)]
        xT = [area(EW + 2064 + s * 512, JX, C) for s in range(2)]
        silu = [area(EW + 3088 + s * 512, DE) for s in range(2)]
        hid = [area(EW + 4112 + s * 512, DE) for s in range(2)]
        hidT = [area(EW + 5136 + s * 256, JH, C) for s in range(2)]
        y_rows = [area(EW + 5648 + s * D, D) for s in range(2)]
        PAD_AT = 30760
        OV = 38800
        y_back = [[area((2 * t + c) * D, D) for c in range(2)] for t in range(NT)]

        one_hot_bf = sb("one_hot_bf", [P, NT, NE], BF16)
        count = sb("count", [P, NE])
        start = sb("start", [P, NE])
        start_i = sb("start_i", [P, NE], I32)
        item = sb("item", [P, 3, NOV])
        item_i = sb("item_i", [P, 2, NOV], I32)
        n_item_i = sb("n_item_i", [P, 1], I32)
        place_i = sb("place_i", [P, NT, 2], U32)
        row_i = [sb(f"row_i{s}", [P, 1], U32) for s in range(2)]
        row_w = [sb(f"row_w{s}", [P, 1]) for s in range(2)]
        row_meta = [sb(f"row_meta{s}", [P, 5]) for s in range(2)]
        row_tmp = sb("row_tmp", [P, 6])

        ps = ctx.enter_context(nc.psum_tensor("ps", [P, 8, 512], F32))

        def cc(name, *shape):
            at, n = CONST[name]
            return split(const[:, at:at + n], shape or (n,))

        ident = cc("ident")
        ident_bf, before_bf, ones_bf = (cbf[:, n * P:(n + 1) * P] for n in range(3))
        band = cbf[:, 3 * P:].rearrange("p (v k) -> p v k", v=NKV)

        sorted_rows = nc.dram_tensor("sorted_rows", (ROWS_SORTED + C, XW), F32, kind="Internal").ap()
        y_dram = nc.dram_tensor("y_dram", (2 * T, D), F32, kind="Internal").ap()

        const_in = sem("const_in")
        route_in = sem("route_in")
        gffn_in = sem("gffn_in")
        x_in = [sem(f"x_in{t}") for t in range(NT)]
        cache_in = sem("cache_in")
        state_in = sem("state_in")
        w_full = [sem(f"w_full{s}") for s in range(2)]
        w_used = sem("w_used")
        zeros_set = sem("zeros_set")
        act_own = sem("act_own")
        dve_own = sem("dve_own")
        pool_own = sem("pool_own")
        ssq_ready = sem("ssq_ready")
        root_ready = sem("root_ready")
        xs_ready = sem("xs_ready")
        xsT_ready = sem("xsT_ready")
        hT_ready = sem("hT_ready")
        z_ready = sem("z_ready")
        z_sq_ready = sem("z_sq_ready")
        z_taken = sem("z_taken")
        z_sum_ready = sem("z_sum_ready")
        z_root_ready = sem("z_root_ready")
        rot_ready = sem("rot_ready")
        rotT_ready = sem("rotT_ready")
        rotT_taken = sem("rotT_taken")
        pastT_ready = sem("pastT_ready")
        pastT_taken = sem("pastT_taken")
        kcT_ready = sem("kcT_ready")
        kcT_taken = sem("kcT_taken")
        u_ready = sem("u_ready")
        u_taken = sem("u_taken")
        pooled_ready = sem("pooled_ready")
        s_ready = sem("s_ready")
        nmax_ready = sem("nmax_ready")
        exp_ready = sem("exp_ready")
        p_ready = sem("p_ready")
        pT_ready = sem("pT_ready")
        pT_taken = [sem("pT_taken_dve"), sem("pT_taken_act")]
        o_ready = sem("o_ready")
        o_taken = sem("o_taken")
        nu_ready = sem("nu_ready")
        nu_taken = sem("nu_taken")
        mix_ready = sem("mix_ready")
        mix_taken = sem("mix_taken")
        gates_ready = sem("gates_ready")
        branch_ready = sem("branch_ready")
        sig_ready = sem("sig_ready")
        gated_own = sem("gated_own")
        merged_ready = sem("merged_ready")
        wo_in = sem("wo_in")
        out_ready = sem("out_ready")
        x2_ready = sem("x2_ready")
        ssq2_ready = sem("ssq2_ready")
        root2_ready = sem("root2_ready")
        hn_ready = sem("hn_ready")
        hnT_ready = sem("hnT_ready")
        hnT_taken = [sem("hnT_taken_dve"), sem("hnT_taken_act")]
        logit_ready = sem("logit_ready")
        diff_ready = sem("diff_ready")
        gexp_ready = sem("gexp_ready")
        choice_ready = sem("choice_ready")
        count_ready = sem("count_ready")
        place_ready = sem("place_ready")
        pad_out = sem("pad_out")
        sorted_out = sem("sorted_out")
        item_ready = sem("item_ready")
        gu_full = [sem(f"gu_full{s}") for s in range(NSLOT)]
        dn_full = [sem(f"dn_full{s}") for s in range(NSLOT)]
        xr_full = [sem(f"xr_full{s}") for s in range(2)]
        xe_ready = sem("xe_ready")
        xe_taken = sem("xe_taken")
        gu_ready = sem("gu_ready")
        silu_ready = sem("silu_ready")
        hid_ready = sem("hid_ready")
        hidT_ready = sem("hidT_ready")
        hidT_taken = sem("hidT_taken")
        dn_ready = sem("dn_ready")
        y_taken = [sem("y_taken_dve"), sem("y_taken_act")]
        row_own = sem("row_own")
        row_i_ready = sem("row_i_ready")
        y_out = [sem(f"y_out{s}") for s in range(2)]
        passed_pe, passed_pool, passed_sp = (sem(f"passed_{e}") for e in ("pe", "pool", "sp"))
        kv_out = sem("kv_out")
        nu_out = sem("nu_out")
        back_in = [sem(f"back_in{t}") for t in range(NT)]
        fin_ready = sem("fin_ready")
        fin_out = sem("fin_out")

        N_CONST = 9
        w_in = a["w_in"]
        STEPS = (NE - 2) // UNROLL

        def slot(n, *shape):
            return area(w_slot[n % 2], *shape)

        def head_groups():
            for n in range(8):
                b, g = n // 2, n % 2
                yield n, b, 4 * g, (P if b == 0 else 2 * P), ([0] if b == 0 else [b - 1, b])

        turns = [(n, kb, v) for n, b, g, w, tiles in head_groups() for kb in range(len(tiles)) for v in range(NKV)]
        first_turn = [next(k for k, tn in enumerate(turns) if tn[0] == n) for n in range(8)] + [len(turns)]
        assert len(turns) % 2 == 0

        def take_probsT(eng, copy, k):
            eng.wait_ge(pT_ready, k + 1)
            n = turns[k][0] if k < len(turns) else 8 + k - len(turns)
            above(eng, o_ready, n)
            w = 512 if k < len(turns) else 256
            copy(probsT[k % 4][:, 0:w], ps[:, 4 + k % 2, 0:w]).then_inc(pT_taken[k % 2], 1)

        def scratch():
            at = [R]

            def take(*shape):
                n = int(np.prod(shape))
                at[0] += n
                assert at[0] <= R + 2048
                return area(at[0] - n, *shape)
            return take

        take = scratch()
        logits = take(NT, NG + NE)
        g_diff, g_exp = take(NT, NG), take(NT, NG)
        e_diff, e_exp = take(NT), take(NT)
        route_exp = [(g_diff, g_exp), (e_diff, e_exp)]
        g_hot, g_tmp = take(NT, NG), take(NT, NG)
        picked, e_tmp, e_hot1, e_hot2 = (take(NT, EG) for _ in range(4))
        wide, hot1, hot2 = (take(NT, NE) for _ in range(3))
        vec = [take(NT) for _ in range(6)]
        cum = [take(2 * NE) for _ in range(2)]

        block = ctx.enter_context(nc.Block())

        @block.sync
        def _(sp):
            def k_major(v):
                return v.rearrange("(k p) n -> p k n", p=P)

            sp.dma_start(const[:], a["const"]).then_inc(const_in, 16)
            sp.dma_start(x[:, 0, :], a["x"][0:P, :]).then_inc(x_in[0], 16)
            sp.dma_start(g_mix[:], a["g_mix"]).then_inc(const_in, 16)
            for t in range(1, NT):
                sp.dma_start(x[0:ROWS[t], t, :], a["x"][t * P:t * P + ROWS[t], :]).then_inc(x_in[t], 16)
            sp.dma_start(slot(0, KD, 256), k_major(w_in[:, KV_OFF:U_OFF])).then_inc(w_full[0], 16)
            sp.dma_start(p_scale[:], a["p_scale"]).then_inc(const_in, 16)
            sp.dma_start(g_qk[:, 0, :], a["gq"].partition_broadcast(P)).then_inc(const_in, 16)
            sp.dma_start(g_qk[:, 1, :], a["gk"].partition_broadcast(P)).then_inc(const_in, 16)
            sp.dma_start(sinks[:].rearrange("p v i -> p (v i)"), a["sinks"].partition_broadcast(P)).then_inc(const_in, 16)
            sp.dma_start(dec_sink[:, 0:1], a["dec_sinks"]).then_inc(const_in, 16)
            sp.dma_start(r_bias[:, 0:NG], a["b_group"].partition_broadcast(P)).then_inc(const_in, 16)
            sp.dma_start(r_bias[:, NG:], a["b_expert"].partition_broadcast(P)).then_inc(const_in, 16)
            for g in range(2):
                if g == 1:
                    sp.wait_ge(w_used, 1)
                dst = slot(1 + g, KD, NKV, 256)
                for v in range(NKV):
                    at = v * 512 + g * 256
                    sp.dma_start(dst[:, :, v, :], k_major(w_in[:, at:at + 256])).then_inc(w_full[(1 + g) % 2], 16)
            sp.dma_start(w_route[:, :, 0:NG], k_major(a["w_group"])).then_inc(route_in, 16)
            sp.dma_start(w_route[:, :, NG:], k_major(a["w_expert"])).then_inc(route_in, 16)
            sp.dma_start(past_u[0:DEC_B * PAST_U, :], a["state"].rearrange("b s c -> (b s) c")).then_inc(state_in, 16)
            sp.dma_start(kc_rows, a["cache_k"].rearrange("b w c -> w b c")).then_inc(cache_in, 16)
            sp.dma_start(vc_rows, a["cache_v"].rearrange("b w c -> w b c")).then_inc(cache_in, 16)
            for n in range(3, 5):
                sp.wait_ge(w_used, n - 1)
                at = U_OFF + 512 * (n - 3)
                sp.dma_start(slot(n, KD, 512), k_major(w_in[:, at:at + 512])).then_inc(w_full[n % 2], 16)
            sp.wait_ge(w_used, 4)
            sp.dma_start(slot(5, KD, 256), k_major(a["w_mix"])).then_inc(w_full[1], 16)

            def load_merge(m, s):
                cols = bass.ts(m, P)
                dst = area(w_slot[s], 4, KD, P)
                for j, off in ((0, GA_OFF), (1, GP_OFF)):
                    sp.dma_start(dst[:, j], k_major(w_in[:, off:off + D])[:, :, cols]).then_inc(w_full[s], 16)
                att = a["w_attn"].rearrange("(v i d) n -> v d i n", v=NKV, i=NI)
                for v in range(NKV):
                    sp.dma_start(dst[64 * v:64 * v + 64, 2], att[v][:, :, cols]).then_inc(w_full[s], 16)
                sp.dma_start(dst[:, 3], k_major(a["w_pool"])[:, :, cols]).then_inc(w_full[s], 16)

            sp.wait_ge(w_used, 5)
            load_merge(0, 0)
            sp.wait_ge(w_used, 6)
            load_merge(1, 1)
            sp.wait_ge(o_taken, 12)
            sp.wait_ge(kv_out, 16 * 6)
            sp.wait_ge(nu_out, 16 * 3)
            for kk in range(2):
                sp.dma_start(w_out[:, 4 * kk:4 * kk + 4, :], k_major(a["w_out"])[:, 4 * kk:4 * kk + 4, :])\
                  .then_inc(wo_in, 16)
            with sp.Fori(0, KD // 2 - 1) as it:
                for s in range(2):
                    m = it * 2 + s
                    sp.wait_ge(branch_ready, m * 2 + 2)
                    load_merge(m + 2, s)

            def load_gu(e, s):
                sp.dma_start(w_up[s], a["w_eu"][bass.ds(e, 1)].squeeze(0)).then_inc(gu_full[s], 16)
                sp.dma_start(w_gate[s], a["w_eg"][bass.ds(e, 1)].squeeze(0)).then_inc(gu_full[s], 16)

            def load_down(e, s):
                sp.dma_start(w_down[s], a["w_ed"][bass.ds(e, 1)].squeeze(0)).then_inc(dn_full[s], 16)

            def load_x(first, s):
                sp.dma_start(x_rows[s][0:C, :], sorted_rows[bass.ds(first, C), :]).then_inc(xr_full[s], 16)

            sp.wait_ge(branch_ready, 2 * KD)
            sp.dma_start(g_ffn, a["g_ffn"].partition_broadcast(P)).then_inc(gffn_in, 16)
            for s in range(NSLOT):
                load_gu(s, s)
                if s < NSLOT - 1:
                    load_down(s, s)
            sp.wait_ge(place_ready, 1)
            load_down(NSLOT - 1, NSLOT - 1)
            sp.wait_ge(sorted_out, 16 * 2 * NT)
            sp.wait_ge(pad_out, 32)
            for e in range(3):
                if e > 1:
                    sp.wait_ge(xe_taken, 1)
                load_x(sp.value_load(start_i[0:1, e:e + 1], min_val=0, max_val=ROWS_SORTED), e % 2)

            def follow(e, k, rows_left=True):
                sp.wait_ge(gu_ready, e + 1)
                sp.sem_inc(passed_sp, 1)
                if rows_left:
                    sp.wait_ge(xe_taken, e + 2)
                    sp.sem_inc(passed_sp, 1)
                    first = sp.value_load(start_i[0:1, bass.ds(e + 3, 1)], min_val=0, max_val=ROWS_SORTED)
                    load_x(first, (k + 1) % 2)
                load_gu(e + NSLOT, k % NSLOT)
                sp.wait_ge(dn_ready, e + 1)
                load_down(e + NSLOT, k % NSLOT)

            with sp.Fori(0, (NE - NSLOT) // UNROLL - 1) as it:
                for k in range(UNROLL):
                    follow(it * UNROLL + k, k)
            for k in range(UNROLL):
                follow(NE - NSLOT - UNROLL + k, k, rows_left=NE - NSLOT - UNROLL + k + 3 < NE)

            sp.wait_ge(item_ready, 1)
            sp.wait_ge(dn_ready, NE)
            n_item = sp.value_load(n_item_i[0:1, 0:1], min_val=0, max_val=NOV)
            with sp.If(n_item > 0):
                with sp.Fori(0, n_item) as i:
                    expert = sp.value_load(item_i[0:1, 0, bass.ds(i, 1)], min_val=0, max_val=NE - 1)
                    first = sp.value_load(item_i[0:1, 1, bass.ds(i, 1)], min_val=0, max_val=ROWS_SORTED)
                    load_x(first, 0)
                    load_gu(expert, 0)
                    load_down(expert, 0)
                    sp.wait_ge(y_out[0], i * 16 + 16 * (NE // 2 + 1))
                    sp.sem_inc(passed_sp, 1)

            for s in range(2):
                sp.wait_ge(y_out[s], 16 * (NE // 2))
            for t in range(NT):
                r = ROWS[t]
                for c in range(2):
                    sp.dma_start(y_back[t][c][0:r, :], y_dram[c * T + t * P:c * T + t * P + r, :])\
                      .then_inc(back_in[t], 16)
            for t in range(NT):
                sp.wait_ge(fin_ready, 2 * t + 2)
                sp.dma_start(o["y"][t * P:t * P + ROWS[t], :], x[0:ROWS[t], t, :]).then_inc(fin_out, 16)
            sp.wait_ge(fin_out, 16 * NT)

        @block.gpsimd
        def _(pool):
            pool.memset(kT_pad[:], 0.0).then_inc(zeros_set, 1)
            pool.memset(kcT_pad, 0.0).then_inc(zeros_set, 1)
            pool.memset(uT[:, :, 0:UP], 0.0).then_inc(zeros_set, 1)
            for m in range(KD):
                pool.memset(split(uT[:, m, UP + SEQ:], (DEC_B, USEG))[:, :, 0:1], 0.0).then_inc(zeros_set, 1)
            pool.memset(eps[:], EPS).then_inc(zeros_set, 1)
            for q in range(1, 4):
                pool.wait_ge(zeros_set, KD + 3 + q)
                pool.memset(v_rows[32 * q:32 * q + 32, 4, :], 0.0).then_inc(zeros_set, 1)
            pool.wait_ge(zeros_set, KD + 7)
            pool.dma_start(o["ks"][:, 0:WIN - DEC_S, :], a["cache_k"][:, DEC_S:, :]).then_inc(kv_out, 16)
            pool.dma_start(o["vs"][:, 0:WIN - DEC_S, :], a["cache_v"][:, DEC_S:, :]).then_inc(kv_out, 16)
            pool.dma_start(o["us"][:, 0:PAST_U - DEC_S, :], a["state"][:, DEC_S:, :]).then_inc(nu_out, 16)
            pool.wait_ge(rot_ready, NT)
            pool.wait_ge(z_taken, NT)
            pool.dma_start(o["kp"], k_rows[:, 3, :]).then_inc(kv_out, 16)
            pool.dma_start(o["vp"], v_rows[:, 3, :]).then_inc(kv_out, 16)
            pool.dma_start(o["ks"][:, WIN - DEC_S:, :], k_rows[0:DEC, 4, :]).then_inc(kv_out, 16)
            pool.dma_start(o["vs"][:, WIN - DEC_S:, :], v_rows[0:DEC, 4, :]).then_inc(kv_out, 16)
            pool.wait_ge(nu_taken, 2)
            pool.dma_start(o["up"], new_u[0:PAST_U, 0, :]).then_inc(nu_out, 16)
            pool.dma_start(o["us"][:, PAST_U - DEC_S:, :], new_u[0:DEC, 1, :]).then_inc(nu_out, 16)
            pool.wait_ge(nu_out, 48)
            pad = area(PAD_AT, XW // 4)
            pool.memset(pad, 0.0).then_inc(pool_own, 1)
            pool.wait_ge(pool_own, 1)
            quarters = sorted_rows[ROWS_SORTED:, :].rearrange("c (q n) -> (c q) n", q=4)
            for h in range(2):
                pool.dma_start(quarters[h * P:(h + 1) * P, :], pad).then_inc(pad_out, 16)
            pool.wait_ge(place_ready, 1)
            for t in range(NT):
                r = ROWS[t]
                for c in range(2):
                    pool.indirect_dma_start(
                        out=sorted_rows, out_offset=bass.IndirectOffsetOnAxis(ap=place_i[0:r, t, c:c + 1], axis=0),
                        in_=hn[0:r, t, :], in_offset=None).then_inc(sorted_out, 16)

            def put_y(e, s):
                pool.wait_ge(y_taken[0], e + 1)
                pool.wait_ge(y_taken[1], e + 1)
                pool.wait_ge(row_i_ready, e + 1)
                pool.sem_inc(passed_pool, 1)
                pool.indirect_dma_start(
                    out=y_dram, out_offset=bass.IndirectOffsetOnAxis(ap=row_i[s][0:C, :], axis=0),
                    in_=y_rows[s][0:C, :], in_offset=None, bounds_check=2 * T - 1, oob_is_err=False)\
                    .then_inc(y_out[s], 16)

            with pool.Fori(0, NE // 2) as it:
                for s in range(2):
                    put_y(it * 2 + s, s)
            pool.wait_ge(item_ready, 1)
            n_item = pool.value_load(n_item_i[0:1, 0:1], min_val=0, max_val=NOV)
            with pool.If(n_item > 0):
                with pool.Fori(0, n_item) as i:
                    put_y(i + NE, 0)

        @block.scalar
        def _(act):
            def copy(out, in_):
                return act.activation(out, in_, ACT.Copy)

            act.wait_ge(zeros_set, 3 + KD + 4)
            for t in range(NT):
                r = ROWS[t]
                act.wait_ge(x_in[t], 16)
                act.activation(x_sq[0:r, :], x[0:r, t, :], ACT.Square, accum_out=stat[0:r, 0, t:t + 1])\
                   .then_inc(ssq_ready, 1)
                act.wait_ge(ssq_ready, t + 1)
                act.activation(stat[0:r, 1, t:t + 1], stat[0:r, 0, t:t + 1], ACT.Sqrt, bias=eps[0:r, :],
                               scale=1.0 / D).then_inc(root_ready, 1)

            for n in range(3 * NT):
                u, t = n // NT, n % NT
                r, s, bank = ROWS[t], n % 2, 4 + n % 4
                w = P if u == 0 else 512
                act.wait_ge(z_ready, n + 1)
                above(act, rot_ready, n - 1)
                act.activation(z_sq[s][0:r, 0:w], ps[0:r, bank, 0:w], ACT.Square).then_inc(z_sq_ready, 1)
                if u == 0:
                    copy(v_rows[0:r, t, :], ps[0:r, bank, P:2 * P])
                copy(z_raw[s][0:r, 0:w], ps[0:r, bank, 0:w]).then_inc(z_taken, 1)
                act.wait_ge(z_sum_ready, n + 1)
                act.activation(z_stat[0:r, s, 1, 0:w // HD], z_stat[0:r, s, 0, 0:w // HD], ACT.Sqrt,
                               bias=eps[0:r, :], scale=1.0 / HD).then_inc(z_root_ready, 1)

            for m in range(KD):
                act.wait_ge(u_ready, m + 1)
                bank = 2 * (m % 4)
                copy(uT[:, m, UP:UP + HALF], ps[:, bank, 0:HALF])
                copy(uT[:, m, UP + HALF:UP + SEQ], ps[:, bank + 1, 0:SEQ - HALF])
                copy(u_decT[:, m, :], ps[:, bank + 1, SEQ - HALF:HALF])
                copy(split(uT[:, m, UP + SEQ:], (DEC_B, USEG))[:, :, UP:],
                     split(ps[:, bank + 1, SEQ - HALF:HALF], (DEC_B, DEC_S))).then_inc(u_taken, 1)

            def exponentials(n, w):
                act.wait_ge(nmax_ready, n + 1)
                s = n % 2
                pb = split(probs[s][:, 0:8 * w], (4, NKV, w))
                for i in range(4):
                    for v in range(NKV):
                        c = i * NKV + v
                        act.activation(pb[:, i, v, :], ps[:, i, v * w:(v + 1) * w], ACT.Exp,
                                       bias=a_stat[:, s, 0, c:c + 1], accum_out=a_stat[:, s, 1, c:c + 1])
                act.activation(a_stat[:, s, 3, :], a_stat[:, s, 2, :], ACT.Exp).then_inc(exp_ready, 1)

            groups = list(head_groups())
            exponentials(0, P)
            for n, b, i0, w, tiles in groups:
                for k in range(first_turn[n], first_turn[n + 1]):
                    if k % 2 == 1:
                        take_probsT(act, copy, k)
                if n < 7:
                    exponentials(n + 1, groups[n + 1][3])
                act.wait_ge(o_ready, n + 1)
                copy(attnT[:, i0:i0 + 4, b * P:(b + 1) * P], split(ps[:, 6 + n % 2, :], (4, P))).then_inc(o_taken, 1)
            act.wait_ge(nmax_ready, 9)
            for g in range(4):
                act.activation(d_probs[:, g, 0:160], d_probs[:, g, 0:160], ACT.Exp, bias=d_stat[:, 0, g:g + 1],
                               accum_out=d_stat[:, 1, g:g + 1])
            act.activation(d_stat[:, 3, :], d_stat[:, 2, :], ACT.Exp).then_inc(exp_ready, 1)
            for g in range(4):
                if g % 2 == 1:
                    take_probsT(act, copy, len(turns) + g)
                act.wait_ge(o_ready, 9 + g)
                for bb in range(2):
                    at = SEQ + (2 * g + bb) * DEC_S
                    ins = copy(attnT[:, :, at:at + DEC_S],
                               split(ps[:, 6 + g % 2, 32 * bb:32 * bb + 32], (NI, DEC_S)))
                ins.then_inc(o_taken, 1)

            for m in range(KD):
                act.wait_ge(mix_ready, m + 1)
                for h in range(2):
                    ins = act.activation(mixedT[:, m, h * HALF:(h + 1) * HALF],
                                         ps[:, 4 + 2 * (m % 2) + h, 0:HALF], ACT.Copy, scale=p_scale[:, m:m + 1])
                ins.then_inc(mix_taken, 1)

            def sigmoids(q, h, first=False):
                act.wait_ge(gates_ready, q + 1)
                if not first:
                    act.wait_ge(merged_ready, q - 1)
                for j in range(2):
                    ins = act.activation(gates[h][j], ps[:, 4 * h + j, 0:HALF], ACT.Sigmoid)
                ins.then_inc(sig_ready, 1)

            for h in range(2):
                sigmoids(h, h, first=True)
            with act.Fori(1, KD) as m:
                for h in range(2):
                    sigmoids(m * 2 + h, h)

            def take_hnT(t):
                act.wait_ge(hnT_ready, t + 1)
                above(act, logit_ready, t - 1)
                r = ROWS[t]
                copy(hnT[t % 2][:, 4:8, 0:r], split(ps[:, 5, :], (4, P))[:, :, 0:r]).then_inc(hnT_taken[1], 1)

            for t in range(NT):
                r = ROWS[t]
                act.wait_ge(x2_ready, t + 1)
                act.activation(hn[0:r, t, 0:D], x[0:r, t, :], ACT.Square, accum_out=stat[0:r, 0, t:t + 1])\
                   .then_inc(ssq2_ready, 1)
                act.wait_ge(ssq2_ready, t + 1)
                act.activation(stat[0:r, 1, t:t + 1], stat[0:r, 0, t:t + 1], ACT.Sqrt, bias=eps[0:r, :],
                               scale=1.0 / D).then_inc(root2_ready, 1)
                if t:
                    take_hnT(t - 1)
            take_hnT(NT - 1)
            for n in range(2):
                act.wait_ge(diff_ready, n + 1)
                t_in, t_out = route_exp[n]
                act.activation(t_out, t_in, ACT.Exp).then_inc(gexp_ready, 1)

            def take_hidT(e, s):
                act.wait_ge(hidT_ready, e + 1)
                copy(hidT[s], split(ps[:, 4 + s, 0:JH * C], (JH, C))).then_inc(hidT_taken, 1)

            def do_silu(e, s):
                act.wait_ge(gu_ready, e + 1)
                act.activation(silu[s][0:C, :], ps[64:64 + C, 2 + s, :], ACT.Silu).then_inc(silu_ready, 1)

            def take_y(e, s, before):
                act.wait_ge(dn_ready, e + 1)
                above(act, y_out[s], before * 16)
                copy(y_rows[s][0:C, 512:1024], ps[64:64 + C, 6 + s, :]).then_inc(y_taken[1], 1)

            def step(e, k, half):
                s = k % 2
                take_hidT(e - 1, 1 - s)
                do_silu(e, s)
                take_y(e - 1, 1 - s, half - (1 - s))

            do_silu(0, 0)
            for k in range(1, 1 + UNROLL):
                step(k, k, k // 2)
            with act.Fori(1, STEPS) as it:
                for k in range(1, 1 + UNROLL):
                    step(it * UNROLL + k, k, it * (UNROLL // 2) + k // 2)
            step(NE - 1, 1, (NE - 1) // 2)
            take_hidT(NE - 1, 1)
            take_y(NE - 1, 1, NE // 2 - 1)
            act.wait_ge(item_ready, 1)
            n_item = act.value_load(n_item_i[0:1, 0:1], min_val=0, max_val=NOV)
            with act.If(n_item > 0):
                with act.Fori(0, n_item) as i:
                    do_silu(i + NE, 0)
                    take_hidT(i + NE, 0)
                    take_y(i + NE, 0, i + NE // 2)

        @block.vector
        def _(dve):
            own = [0]

            def link(ins):
                own[0] += 1
                ins.then_inc(dve_own, 1)
                dve.wait_ge(dve_own, own[0])

            def over(v, n):
                return v.unsqueeze(2).to_broadcast((v.shape[0], v.shape[1], n))

            def across(v, n):
                return v.unsqueeze(1).to_broadcast((v.shape[0], n, v.shape[1]))

            tt, ts, stt = dve.tensor_tensor, dve.tensor_scalar, dve.scalar_tensor_tensor
            dve.wait_ge(const_in, 16 * N_CONST)
            dve.wait_ge(zeros_set, 3 + KD + 4)
            for c in range(2):
                g = g_qk[:, c, :]
                for half in range(2):
                    own_half, other = slice(32 * half, 32 * half + 32), slice(32 - 32 * half, 64 - 32 * half)
                    tt(rot[:, 2 * c, :, own_half], cc("cos", NT, 32), across(g[:, own_half], NT), ALU.mult)
                    link(tt(rot[:, 2 * c + 1, :, own_half], cc("sin", NT, 32), across(g[:, other], NT), ALU.mult))
                link(ts(rot[:, 2 * c + 1, :, 0:32], rot[:, 2 * c + 1, :, 0:32], -1.0, None, ALU.mult))
            dve.tensor_copy(ident_bf, ident)
            dve.tensor_copy(before_bf, cc("before"))
            dve.memset(ones_bf, 1.0)
            for v in range(NKV):
                ins = dve.tensor_copy(band[:, v, :], cc("band"))
            link(ins)
            link(ts(neg_sink[:].rearrange("p i v -> p v i"), sinks[:], -1.0, None, ALU.mult))
            link(ts(dec_sink[:, 1:2], dec_sink[:, 0:1], -1.0, None, ALU.mult))

            for t in range(NT + 1):
                if t < NT:
                    r = ROWS[t]
                    dve.wait_ge(root_ready, t + 1)
                    above(dve, xsT_ready, t - 1)
                    link(dve.reciprocal(stat[0:r, 2, t:t + 1], stat[0:r, 1, t:t + 1]))
                    ts(xs[t % 2][0:r, :], x[0:r, t, :], stat[0:r, 2, t:t + 1], None, ALU.mult).then_inc(xs_ready, 1)
                if t > 0:
                    r, at = ROWS[t - 1], (t - 1) * P
                    dve.wait_ge(xsT_ready, t)
                    for kk in range(2):
                        ins = tt(hT[:, 4 * kk:4 * kk + 4, at:at + r],
                                 split(ps[:, 2 * ((t - 1) % 2) + kk, :], (4, P))[:, :, 0:r],
                                 over(g_mix[:, 4 * kk:4 * kk + 4], r), ALU.mult)
                    ins.then_inc(hT_ready, 1)

            def take_rotT(n):
                u, t = n // NT, n % NT
                r, at = ROWS[t], t * P
                dve.wait_ge(rotT_ready, n + 1)
                if u == 0:
                    for v in range(NKV):
                        rows = slice(64 * v, 64 * v + 64)
                        ins = dve.tensor_copy(kT_pad[rows, v, at:at + r], ps[rows, n % 2, 0:r])
                elif t < NT - 1:
                    ins = ts(qT[:, 4 * (u - 1):4 * u, at:at + r], split(ps[:, n % 2, :], (4, P)),
                             float(HD) ** -0.5, None, ALU.mult)
                else:
                    for i in range(4):
                        ins = ts(q_decT[:, :, 4 * (u - 1) + i, :], split(ps[:, n % 2, i * P:i * P + r], (DEC_B, DEC_S)),
                                 float(HD) ** -0.5, None, ALU.mult)
                ins.then_inc(rotT_taken, 1)

            for n in range(3 * NT):
                u, t = n // NT, n % NT
                r, s = ROWS[t], n % 2
                heads = 2 if u == 0 else 8
                w = heads * HD
                raw, norm, own_part, other_part = (split(v[0:r, 0:w], (heads, HD)) for v in
                                                   (z_raw[s], z_norm, z_cos, z_sin))
                tables = [across(rot[0:r, (2 if u == 0 else 0) + c, t, :], heads) for c in range(2)]
                dve.wait_ge(z_sq_ready, n + 1)
                dve.tensor_reduce(z_stat[0:r, s, 0, 0:heads], split(z_sq[s][0:r, 0:w], (heads, HD)), AX_X, ALU.add)\
                   .then_inc(z_sum_ready, 1)
                dve.wait_ge(z_root_ready, n + 1)
                dve.wait_ge(z_taken, n + 1)
                link(dve.reciprocal(z_stat[0:r, s, 2, 0:heads], z_stat[0:r, s, 1, 0:heads]))
                link(tt(norm, raw, over(z_stat[0:r, s, 2, 0:heads], HD), ALU.mult))
                tt(own_part, norm, tables[0], ALU.mult)
                tt(other_part[:, :, 0:32], norm[:, :, 32:64], tables[1][:, :, 0:32], ALU.mult)
                link(tt(other_part[:, :, 32:64], norm[:, :, 0:32], tables[1][:, :, 32:64], ALU.mult))
                above(dve, rotT_ready, n - 1)
                if u == 0:
                    ins = tt(split(k_rows[0:r, t, :], (heads, HD)), own_part, other_part, ALU.add)
                else:
                    out = split(q_rows[s][0:r, :], (4, NKV, HD)).rearrange("p i v d -> p v i d")
                    ins = tt(out, split(z_cos[0:r, :], (NKV, 4, HD)), split(z_sin[0:r, :], (NKV, 4, HD)), ALU.add)
                ins.then_inc(rot_ready, 1)
                if n:
                    take_rotT(n - 1)
            take_rotT(3 * NT - 1)

            dve.wait_ge(pastT_ready, 1)
            for m in range(KD):
                ins = dve.tensor_copy(split(uT[:, m, UP + SEQ:], (DEC_B, USEG))[:, :, 1:UP],
                                      split(ps[:, 2 + m // 4, (m % 4) * P:(m % 4) * P + DEC_B * PAST_U], (DEC_B, PAST_U)))
            ins.then_inc(pastT_taken, 1)
            dve.wait_ge(kcT_ready, 1)
            for kk in range(2):
                for v in range(NKV):
                    rows = slice(64 * v, 64 * v + 64)
                    ins = dve.tensor_copy(kcT_pad[rows, 4 * kk:4 * kk + 4, v, :], split(ps[rows, 4 + kk, :], (4, P)))
            ins.then_inc(kcT_taken, 1)

            for g, width in enumerate(POOL_W):
                dve.wait_ge(u_taken, 2 * g + 2)
                u2 = uT[:, 2 * g:2 * g + 2, :]
                src, n = u2, 1
                for lvl in range(g + 1):
                    dst = win_sum[lvl % 2]
                    link(tt(dst[:, :, 2 * n - 1:], src[:, :, 2 * n - 1:], src[:, :, n - 1:UW - n], ALU.add))
                    src, n = dst, 2 * n
                out = pooledT[:, 2 * g:2 * g + 2, :]
                link(stt(out[:, :, 0:SEQ], src[:, :, UP:UP + SEQ], 1.0 / width, u2[:, :, UP:UP + SEQ],
                         ALU.mult, ALU.subtract))
                for c in range(2):
                    dec_sum, dec_u = (split(v[:, c, UP + SEQ:], (DEC_B, USEG))[:, :, UP:] for v in (src, u2))
                    stt(split(out[:, c, SEQ:], (DEC_B, DEC_S)), dec_sum, 1.0 / width, dec_u, ALU.mult, ALU.subtract)
                link(tt(out[:, :, 0:16], src[:, :, UP:UP + 16], across(cc("inv_count", 4, 16)[:, g, :], 2), ALU.mult))
                tt(out[:, :, 0:16], out[:, :, 0:16], u2[:, :, UP:UP + 16], ALU.subtract).then_inc(pooled_ready, 1)

            def maxima(n, i0, w):
                s = n % 2
                dve.wait_ge(s_ready, n + 1)
                link(dve.tensor_reduce(split(a_stat[:, s, 0, :], (4, NKV)), ps[:, 0:4, 0:2 * w].rearrange("p i (v k) -> p i v k", v=NKV),
                                       AX_X, ALU.max, negate=True))
                ns = neg_sink[:, i0:i0 + 4, :].rearrange("p i v -> p (i v)")
                link(tt(a_stat[:, s, 0, :], a_stat[:, s, 0, :], ns, ALU.min))
                tt(a_stat[:, s, 2, :], a_stat[:, s, 0, :], ns, ALU.subtract).then_inc(nmax_ready, 1)

            def normalise(n, w):
                s = n % 2
                dve.wait_ge(exp_ready, n + 1)
                link(tt(a_stat[:, s, 1, :], a_stat[:, s, 1, :], a_stat[:, s, 3, :], ALU.add))
                link(dve.reciprocal(a_stat[:, s, 1, :], a_stat[:, s, 1, :]))
                for c in range(8):
                    v = probs[s][:, c * w:(c + 1) * w]
                    ins = ts(v, v, a_stat[:, s, 1, c:c + 1], None, ALU.mult)
                ins.then_inc(p_ready, 1)

            groups = list(head_groups())
            maxima(0, 0, P)
            for n, b, i0, w, tiles in groups:
                normalise(n, w)
                if n < 7:
                    maxima(n + 1, groups[n + 1][2], groups[n + 1][3])
                for k in range(first_turn[n], first_turn[n + 1]):
                    if k % 2 == 0:
                        take_probsT(dve, dve.tensor_copy, k)
            dve.wait_ge(pT_ready, len(turns))
            dve.wait_ge(s_ready, 9)
            link(dve.memset(d_probs[:, :, 160:256], 0.0))
            link(tt(d_probs[:, :, 0:160], ps[:, 0:4, 0:160], cc("dec_mask", 4, 160), ALU.add))
            link(dve.tensor_reduce(d_stat[:, 0, :], d_probs[:, :, 0:160], AX_X, ALU.max, negate=True))
            link(ts(d_stat[:, 0, :], d_stat[:, 0, :], dec_sink[:, 1:2], None, ALU.min))
            ts(d_stat[:, 2, :], d_stat[:, 0, :], dec_sink[:, 0:1], None, ALU.add).then_inc(nmax_ready, 1)
            dve.wait_ge(exp_ready, 9)
            link(tt(d_stat[:, 1, :], d_stat[:, 1, :], d_stat[:, 3, :], ALU.add))
            link(dve.reciprocal(d_stat[:, 1, :], d_stat[:, 1, :]))
            tt(d_probs[:, :, 0:160], d_probs[:, :, 0:160], over(d_stat[:, 1, :], 160), ALU.mult).then_inc(p_ready, 1)
            for g in range(0, 4, 2):
                take_probsT(dve, dve.tensor_copy, len(turns) + g)
            dve.wait_ge(nu_ready, 1)
            dve.tensor_copy(new_u[0:PAST_U, 0, :].rearrange("p (b n) -> p b n", b=2), ps[0:PAST_U, 0:2, :]).then_inc(nu_taken, 1)
            dve.tensor_copy(new_u[0:DEC, 1, :].rearrange("p (b n) -> p b n", b=2), ps[0:DEC, 2:4, :]).then_inc(nu_taken, 1)

            def merge(m, q, h):
                dve.wait_ge(sig_ready, q + 1)
                dve.wait_ge(branch_ready, q + 1)
                for j in range(2):
                    tt(gated[h][j], gates[h][j], ps[:, 4 * h + 2 + j, 0:HALF], ALU.mult).then_inc(gated_own, 1)
                dve.wait_ge(gated_own, q * 2 + 2)
                out = mergedT[:, bass.ds(m, 1), h * HALF:(h + 1) * HALF].squeeze(1)
                tt(out, gated[h][0], gated[h][1], ALU.add).then_inc(merged_ready, 1)

            with dve.Fori(0, KD) as m:
                for h in range(2):
                    merge(m, m * 2 + h, h)

            def take_hnT(t):
                dve.wait_ge(hnT_ready, t + 1)
                above(dve, logit_ready, t - 1)
                r = ROWS[t]
                dve.tensor_copy(hnT[t % 2][:, 0:4, 0:r], split(ps[:, 4, :], (4, P))[:, :, 0:r])\
                   .then_inc(hnT_taken[0], 1)

            dve.wait_ge(gffn_in, 16)
            for t in range(NT):
                r, bank = ROWS[t], 2 * (t % 2)
                dve.wait_ge(out_ready, t + 1)
                xr = x[0:r, t, :]
                tt(split(xr, (2, 512)), ps[0:r, bank:bank + 2, :], split(xr, (2, 512)), ALU.add).then_inc(x2_ready, 1)
                dve.wait_ge(root2_ready, t + 1)
                link(dve.reciprocal(stat[0:r, 2, t:t + 1], stat[0:r, 1, t:t + 1]))
                stt(hn[0:r, t, 0:D], xr, stat[0:r, 2, t:t + 1], g_ffn[0:r, :], ALU.mult, ALU.mult).then_inc(hn_ready, 1)
                if t:
                    take_hnT(t - 1)
            link(dve.memset(logits[:, NT - 1, :], 0.0))
            take_hnT(NT - 1)

            dve.wait_ge(logit_ready, NT)
            rows4 = NT - 1
            tt(logits[:, 0:rows4, :], split(ps[:, 6, 0:NT * 36], (NT, 36))[:, 0:rows4, :], across(r_bias[:], rows4), ALU.add)
            link(tt(logits[0:DEC, rows4, :], split(ps[:, 6, 0:NT * 36], (NT, 36))[0:DEC, rows4, :], r_bias[0:DEC, :], ALU.add))
            gl, el = logits[:, :, 0:NG], logits[:, :, NG:]
            g_max, g_share, e_max1, e_max2, w_first, w_second = vec

            def first_hot(hot, values, best, rank, tmp, n):
                link(tt(tmp, values, over(best, n), ALU.is_equal))
                link(tt(tmp, tmp, across(rank, NT), ALU.mult))
                link(dve.tensor_reduce(w_second, tmp, AX_X, ALU.max))
                link(tt(hot, tmp, over(w_second, n), ALU.is_equal))

            link(dve.tensor_reduce(g_max, gl, AX_X, ALU.max))
            tt(g_diff, gl, over(g_max, NG), ALU.subtract).then_inc(diff_ready, 1)
            first_hot(g_hot, gl, g_max, cc("group_rank"), g_tmp, NG)
            for g in range(NG):
                ins = tt(wide[:, :, g * EG:(g + 1) * EG], el[:, :, g * EG:(g + 1) * EG],
                         g_hot[:, :, g:g + 1].to_broadcast((P, NT, EG)), ALU.mult)
            link(ins)
            link(dve.tensor_reduce(picked, wide.rearrange("p t (g e) -> p t e g", g=NG), AX_X, ALU.add))
            link(dve.tensor_reduce(e_max1, picked, AX_X, ALU.max))
            first_hot(e_hot1, picked, e_max1, cc("expert_rank"), e_tmp, EG)
            link(stt(picked, e_hot1, -3.0e38, picked, ALU.mult, ALU.add))
            link(dve.tensor_reduce(e_max2, picked, AX_X, ALU.max))
            tt(e_diff, e_max2, e_max1, ALU.subtract).then_inc(diff_ready, 1)
            first_hot(e_hot2, picked, e_max2, cc("expert_rank"), e_tmp, EG)
            for g in range(NG):
                cols = slice(g * EG, (g + 1) * EG)
                tt(hot1[:, :, cols], e_hot1, g_hot[:, :, g:g + 1].to_broadcast((P, NT, EG)), ALU.mult)
                ins = tt(hot2[:, :, cols], e_hot2, g_hot[:, :, g:g + 1].to_broadcast((P, NT, EG)), ALU.mult)
            link(ins)
            link(tt(wide, hot1, hot2, ALU.add))
            tt(one_hot_bf[:], wide, over(cc("live"), NE), ALU.mult).then_inc(choice_ready, 1)
            dve.wait_ge(choice_ready, 1)
            for c, hot in ((0, hot1), (1, hot2)):
                link(tt(wide, hot, across(cc("expert_id"), NT), ALU.mult))
                link(dve.tensor_reduce(hn[:, :, D + 1 + 2 * c:D + 2 + 2 * c], wide, AX_X, ALU.add))
            dve.wait_ge(gexp_ready, 2)
            link(dve.tensor_reduce(g_share, g_exp, AX_X, ALU.add))
            link(dve.reciprocal(g_share, g_share))
            link(ts(w_second, e_exp, 1.0, None, ALU.add))
            link(dve.reciprocal(w_second, w_second))
            link(tt(w_first, g_share, w_second, ALU.mult))
            link(tt(w_second, w_first, e_exp, ALU.mult))
            dve.tensor_copy(hn[:, :, D + 2:D + 3], w_first.unsqueeze(2))
            dve.tensor_copy(hn[:, :, D + 4:D + 5], w_second.unsqueeze(2))
            dve.memset(hn[:, :, D + 5:XW], 0.0)
            for t in range(NT):
                ts(hn[:, t, D:D + 1], cc("row"), float(t * P), None, ALU.add)

            def exclusive_sum(out, v, cum):
                link(dve.memset(cum[0][:, 0:NE], 0.0))
                link(dve.memset(cum[1][:, 0:NE], 0.0))
                link(dve.tensor_copy(cum[0][:, NE:], v))
                n, s = 1, 0
                while n < NE:
                    link(tt(cum[1 - s][:, NE:], cum[s][:, NE:], cum[s][:, NE - n:2 * NE - n], ALU.add))
                    n, s = 2 * n, 1 - s
                link(tt(out, cum[s][:, NE:], v, ALU.subtract))

            dve.wait_ge(count_ready, 1)
            link(dve.tensor_copy(count[:], ps[:, 7, 256:256 + NE]))
            exclusive_sum(start[:], count[:], cum)
            link(dve.tensor_copy(start_i[:], start[:]))
            link(tt(wide, split(ps[:, 7, 0:NT * NE], (NT, NE)), across(start[:], NT), ALU.add))
            link(tt(hot1, hot1, wide, ALU.mult))
            link(tt(hot2, hot2, wide, ALU.mult))
            link(dve.tensor_reduce(vec[0], hot1, AX_X, ALU.add))
            link(dve.tensor_reduce(vec[1], hot2, AX_X, ALU.add))
            dve.tensor_copy(place_i[:, :, 0:1], vec[0].unsqueeze(2))
            dve.tensor_copy(place_i[:, :, 1:2], vec[1].unsqueeze(2)).then_inc(place_ready, 1)

            def row_chain(n):
                dve.wait_ge(row_own, n)

            def take_x(e, s, full):
                dve.wait_ge(xr_full[s], full)
                dve.tensor_copy(row_meta[s][0:C, :], x_rows[s][0:C, D:D + 5]).then_inc(row_own, 1)
                dve.wait_ge(xe_ready, e + 1)
                dve.tensor_copy(xT[s], split(ps[:, s, :], (JX, C))).then_inc(xe_taken, 1)

            N_ROW = 8

            def weights(e, s, expert):
                m, t = row_meta[s][0:C, :], row_tmp[0:C, :]
                row_chain(e * N_ROW + 1)
                ts(t[:, 0:1], m[:, 1:2], expert, m[:, 2:3], ALU.is_equal, ALU.mult).then_inc(row_own, 1)
                ts(t[:, 1:2], m[:, 3:4], expert, m[:, 4:5], ALU.is_equal, ALU.mult).then_inc(row_own, 1)
                row_chain(e * N_ROW + 3)
                tt(row_w[s][0:C, :], t[:, 0:1], t[:, 1:2], ALU.add).then_inc(row_own, 1)
                row_chain(e * N_ROW + 4)

            def hidden(e, s):
                dve.wait_ge(silu_ready, e + 1)
                stt(hid[s][0:C, :], ps[0:C, 2 + s, :], row_w[s][0:C, :], silu[s][0:C, :], ALU.mult, ALU.mult)\
                    .then_inc(hid_ready, 1)

            def targets(e, s, expert, left, before):
                m, t = row_meta[s][0:C, :], row_tmp[0:C, :]
                ts(t[:, 2:3], m[:, 3:4], expert, float(T), ALU.is_equal, ALU.mult).then_inc(row_own, 1)
                ts(t[:, 3:4], cc("row")[0:C, :], left, None, ALU.is_lt).then_inc(row_own, 1)
                row_chain(e * N_ROW + 6)
                tt(t[:, 4:5], m[:, 0:1], t[:, 2:3], ALU.add).then_inc(row_own, 1)
                row_chain(e * N_ROW + 7)
                stt(t[:, 5:6], t[:, 4:5], -BIG, t[:, 3:4], ALU.add, ALU.mult).then_inc(row_own, 1)
                row_chain(e * N_ROW + 8)
                above(dve, y_out[s], before * 16)
                ts(row_i[s][0:C, :], t[:, 5:6], BIG, None, ALU.add).then_inc(row_i_ready, 1)

            def take_y(e, s, before):
                dve.wait_ge(dn_ready, e + 1)
                above(dve, y_out[s], before * 16)
                dve.tensor_copy(y_rows[s][0:C, 0:512], ps[0:C, 6 + s, :]).then_inc(y_taken[0], 1)

            def column(table, e):
                return table[0:C, e:e + 1] if isinstance(e, int) else table[0:C, bass.ds(e, 1)]

            def step(e, k, half, last=False):
                s = k % 2
                weights(e, s, column(cc("expert_id"), e))
                hidden(e, s)
                targets(e, s, column(cc("expert_id"), e), column(count[:], e), half)
                if not last:
                    take_x(e + 1, 1 - s, (half + 1 + s) * 16)

                if not isinstance(e, int) or e > 0:
                    take_y(e - 1, 1 - s, half - (1 - s))

            def list_items():
                at = [OV]

                def take(*shape):
                    n = int(np.prod(shape))
                    at[0] += n
                    return area(at[0] - n, *shape)

                more, before, base, left0 = (take(NE) for _ in range(4))
                edges = take(NE, 8)
                cums = [take(2 * NE) for _ in range(2)]
                sel, tmp = take(NOV, NE), take(NOV, NE)
                steps, total = take(NOV), take(1)
                link(tt(edges, over(count[:], 8), across(cc("chunk_edge"), NE), ALU.is_gt))
                link(dve.tensor_reduce(more, edges, AX_X, ALU.add))
                exclusive_sum(before, more, cums)
                link(stt(base, before, -float(C), start[:], ALU.mult, ALU.add))
                link(ts(base, base, float(C), None, ALU.add))
                link(stt(left0, before, float(C), count[:], ALU.mult, ALU.add))
                link(ts(left0, left0, -float(C), None, ALU.add))
                link(tt(sel, over(cc("item"), NE), across(before, NOV), ALU.is_ge))
                link(tt(before, before, more, ALU.add))
                link(tt(tmp, over(cc("item"), NE), across(before, NOV), ALU.is_lt))
                link(tt(sel, sel, tmp, ALU.mult))
                for c, v in enumerate((cc("expert_id"), base, left0)):
                    link(tt(tmp, sel, across(v, NOV), ALU.mult))
                    link(dve.tensor_reduce(item[:, c, :], tmp, AX_X, ALU.add))
                link(ts(steps, cc("item"), float(C), None, ALU.mult))
                link(tt(item[:, 1, :], item[:, 1, :], steps, ALU.add))
                link(tt(item[:, 2, :], item[:, 2, :], steps, ALU.subtract))
                link(dve.tensor_copy(item_i[:], item[:, 0:2, :]))
                link(dve.tensor_reduce(total, more, AX_X, ALU.add))
                dve.tensor_copy(n_item_i[:], total).then_inc(item_ready, 1)

            take_x(0, 0, 16)
            step(0, 0, 0)
            list_items()
            for k in range(1, 1 + UNROLL):
                step(k, k, k // 2)
            with dve.Fori(1, STEPS) as it:
                for k in range(1, 1 + UNROLL):
                    step(it * UNROLL + k, k, it * (UNROLL // 2) + k // 2)
            step(NE - 1, 1, (NE - 1) // 2, last=True)
            take_y(NE - 1, 1, NE // 2 - 1)
            dve.wait_ge(item_ready, 1)
            n_item = dve.value_load(n_item_i[0:1, 0:1], min_val=0, max_val=NOV)
            with dve.If(n_item > 0):
                with dve.Fori(0, n_item) as i:
                    take_x(i + NE, 0, i * 16 + 16 * (NE // 2 + 1))
                    weights(i + NE, 0, item[0:C, 0, bass.ds(i, 1)])
                    hidden(i + NE, 0)
                    targets(i + NE, 0, item[0:C, 0, bass.ds(i, 1)], item[0:C, 2, bass.ds(i, 1)], i + NE // 2)
                    take_y(i + NE, 0, i + NE // 2)
            for t in range(NT):
                r = ROWS[t]
                dve.wait_ge(back_in[t], 32)
                for c in range(2):
                    tt(x[0:r, t, :], x[0:r, t, :], y_back[t][c][0:r, :], ALU.add).then_inc(fin_ready, 1)
                    dve.wait_ge(fin_ready, 2 * t + c + 1)

        @block.tensor
        def _(pe):
            mm, transpose = pe.matmul, pe.transpose

            pe.wait_ge(const_in, 16 * N_CONST)
            for t in range(NT):
                r = ROWS[t]
                pe.wait_ge(xs_ready, t + 1)
                above(pe, hT_ready, t - 1)
                for k in range(KD):
                    ins = transpose(ps[:, 2 * (t % 2) + k // 4, (k % 4) * P:(k % 4) * P + r],
                                    xs[t % 2][0:r, k * P:(k + 1) * P], ident[0:r, 0:r])
                ins.then_inc(xsT_ready, 1)

            def rotT(n):
                u, t = n // NT, n % NT
                r = ROWS[t]
                pe.wait_ge(rot_ready, n + 1)
                above(pe, rotT_taken, n - 1)
                if n < 2:
                    pe.wait_ge(hT_ready, NT)
                if u == 0:
                    transpose(ps[:, n % 2, 0:r], k_rows[0:r, t, :], ident[0:r, 0:r]).then_inc(rotT_ready, 1)
                    return
                for i in range(4):
                    ins = transpose(ps[:, n % 2, i * P:i * P + r], q_rows[n % 2][0:r, i * P:(i + 1) * P], ident[0:r, 0:r])
                ins.then_inc(rotT_ready, 1)

            for n in range(3 * NT):
                u, t = n // NT, n % NT
                r, w, bank = ROWS[t], (256 if u == 0 else 512), 4 + n % 4
                if t == 0:
                    pe.wait_ge(w_full[u % 2], (16, 32, 48)[u])
                if u == 0:
                    pe.wait_ge(hT_ready, t + 1)
                above(pe, z_taken, n - 3)
                for k in range(KD):
                    ins = mm(ps[0:r, bank, 0:w], hT[:, k, t * P:t * P + r], slot(u, KD, w)[:, k, :],
                             start=k == 0, stop=k == KD - 1)
                ins.then_inc(z_ready, 1)
                if n:
                    rotT(n - 1)
                if t == NT - 1:
                    pe.wait_ge(z_ready, n + 1)
                    pe.sem_inc(w_used, 1)
            rotT(3 * NT - 1)

            pe.wait_ge(state_in, 16)
            for m in range(KD):
                ins = transpose(ps[:, 2 + m // 4, (m % 4) * P:(m % 4) * P + DEC_B * PAST_U],
                                past_u[0:DEC_B * PAST_U, m * P:(m + 1) * P], ident[0:DEC_B * PAST_U, 0:DEC_B * PAST_U])
            ins.then_inc(pastT_ready, 1)
            pe.wait_ge(cache_in, 32)
            pe.wait_ge(z_taken, 3 * NT)
            for b in range(DEC_B):
                ins = transpose(ps[:, 4 + b // 4, (b % 4) * P:(b % 4 + 1) * P], kc_rows[:, b, :], ident)
            ins.then_inc(kcT_ready, 1)

            for m in range(KD):
                n = 3 + m // 4
                if m % 4 == 0:
                    pe.wait_ge(w_full[n % 2], (48, 64)[m // 4])
                if m == 0:
                    pe.wait_ge(rotT_taken, 3 * NT)
                if m == 1:
                    pe.wait_ge(pastT_taken, 1)
                if m == 2:
                    pe.wait_ge(kcT_taken, 1)
                above(pe, u_taken, m - 3)
                for h in range(2):
                    for k in range(KD):
                        ins = mm(ps[:, 2 * (m % 4) + h, 0:HALF], slot(n, KD, 512)[:, k, (m % 4) * P:(m % 4 + 1) * P],
                                 hT[:, k, h * HALF:(h + 1) * HALF], start=k == 0, stop=k == KD - 1)
                ins.then_inc(u_ready, 1)
                if m % 4 == 3:
                    pe.wait_ge(u_ready, m + 1)
                    pe.sem_inc(w_used, 1)

            groups = list(head_groups())

            def scores(n):
                _, b, i0, w, tiles = groups[n]
                if n == 0:
                    pe.wait_ge(u_taken, KD)
                above(pe, exp_ready, n)
                for i in range(4):
                    out = ps[:, i, 0:2 * w].rearrange("p (v k) -> p v k", v=NKV)
                    mm(out, qT[:, i0 + i, b * P:(b + 1) * P], kT_pad[:, :, tiles[0] * P:(b + 1) * P],
                       start=True, stop=False)
                    ins = mm(out, ident_bf, band[:, :, 2 * P - w:], start=False, stop=True)
                ins.then_inc(s_ready, 1)

            def probsT_turn(n, k, kb, v, w):
                above(pe, pT_taken[k % 2], k // 2)
                pb = split(probs[n % 2][:, 0:8 * w], (4, NKV, w))
                for i in range(4):
                    ins = transpose(ps[:, 4 + k % 2, i * P:(i + 1) * P], pb[:, i, v, kb * P:(kb + 1) * P], ident)
                ins.then_inc(pT_ready, 1)

            scores(0)
            for n, b, i0, w, tiles in groups:
                if n < 7:
                    scores(n + 1)
                pe.wait_ge(p_ready, n + 1)
                mine = range(first_turn[n], first_turn[n + 1])
                for k in mine:
                    probsT_turn(n, k, turns[k][1], turns[k][2], w)
                above(pe, o_taken, n - 1)
                for k in mine:
                    _, kb, v = turns[k]
                    pe.wait_ge(pT_taken[k % 2], k // 2 + 1)
                    ins = mm(ps[64 * v:64 * v + 64, 6 + n % 2, :], v_rows[:, tiles[kb], 64 * v:64 * v + 64], probsT[k % 4],
                             start=kb == 0, stop=kb == len(tiles) - 1)
                ins.then_inc(o_ready, 1)
            pe.wait_ge(exp_ready, 8)
            for g in range(4):
                for bb in range(2):
                    for v in range(NKV):
                        b, p = 2 * g + bb, 32 * (2 * bb + v)
                        q = q_decT[:, b, :, :].rearrange("p i s -> p (i s)")
                        mm(ps[p:p + 32, g, 0:P], q, kcT_pad[:, b, v, :], start=True, stop=True)
                        ins = mm(ps[p:p + 32, g, P:P + DEC], q, kT_pad[:, v, SEQ:], start=True, stop=True)
            ins.then_inc(s_ready, 1)
            pe.wait_ge(p_ready, 9)
            for g in range(4):
                k = len(turns) + g
                pe.wait_ge(pT_taken[k % 2], k // 2)
                for c in range(2):
                    ins = transpose(ps[:, 4 + k % 2, c * P:(c + 1) * P], d_probs[:, g, c * P:(c + 1) * P], ident)
                ins.then_inc(pT_ready, 1)
                pe.wait_ge(pT_taken[k % 2], k // 2 + 1)
                pe.wait_ge(o_taken, 7 + g)
                for bb in range(2):
                    for v in range(NKV):
                        b, rows, cols = 2 * g + bb, slice(64 * v, 64 * v + 64), slice(32 * bb, 32 * bb + 32)
                        at = 32 * (2 * bb + v)
                        mm(ps[rows, 6 + g % 2, cols], vc_rows[:, b, rows], probsT[k % 4][:, at:at + 32],
                           start=True, stop=False)
                        ins = mm(ps[rows, 6 + g % 2, cols], v_rows[:, 4, rows], probsT[k % 4][:, P + at:P + at + 32],
                                 start=False, stop=True)
                ins.then_inc(o_ready, 1)
            for m in range(KD):
                transpose(ps[0:PAST_U, m // 4, (m % 4) * P:(m % 4 + 1) * P],
                          uT[:, m, UP + SEQ - PAST_U:UP + SEQ], ident)
                ins = transpose(ps[0:DEC, 2 + m // 4, (m % 4) * P:(m % 4 + 1) * P],
                                u_decT[:, m, :], ident)
            ins.then_inc(nu_ready, 1)

            pe.wait_ge(w_full[1], 64)
            pe.wait_ge(pooled_ready, 4)
            pe.wait_ge(pT_taken[0], len(turns) // 2 + 2)
            pe.wait_ge(pT_taken[1], len(turns) // 2 + 2)
            pe.wait_ge(o_taken, 12)
            for m in range(KD):
                g, c = m // 2, m % 2
                above(pe, mix_taken, m - 1)
                for h in range(2):
                    for k in range(2):
                        ins = mm(ps[:, 4 + 2 * c + h, 0:HALF], slot(5, KD, 256)[:, 2 * g + k, c * P:(c + 1) * P],
                                 pooledT[:, 2 * g + k, h * HALF:(h + 1) * HALF], start=k == 0, stop=k == 1)
                ins.then_inc(mix_ready, 1)
            pe.wait_ge(mix_ready, KD)
            pe.sem_inc(w_used, 1)
            pe.wait_ge(mix_taken, KD)
            pe.wait_ge(nu_taken, 2)

            def merge(q, h, s):
                w = area(w_slot[s], 4, KD, P)
                for j, src in enumerate((hT, hT, attnT, mixedT)):
                    for k in range(KD):
                        ins = mm(ps[:, 4 * h + j, 0:HALF], w[:, j, k, :], src[:, k, h * HALF:(h + 1) * HALF],
                                 start=k == 0, stop=k == KD - 1)
                    if j == 1:
                        ins.then_inc(gates_ready, 1)
                ins.then_inc(branch_ready, 1)

            for s in range(2):
                pe.wait_ge(w_full[s], 64 + 80)
                for h in range(2):
                    above(pe, merged_ready, 2 * s + h - 1)
                    merge(2 * s + h, h, s)
            with pe.Fori(1, KD // 2) as it:
                for s in range(2):
                    pe.wait_ge(w_full[s], it * 80 + (64 + 80))
                    for h in range(2):
                        pe.wait_ge(merged_ready, it * 4 + (2 * s + h - 1))
                        merge(it * 4 + (2 * s + h), h, s)

            def rows_out(t):
                r, bank = ROWS[t], 2 * (t % 2)
                above(pe, x2_ready, t - 1)
                for c in range(2):
                    for k in range(KD):
                        ins = mm(ps[0:r, bank + c, :], mergedT[:, k, t * P:t * P + r], w_out[:, k, c * 512:(c + 1) * 512],
                                 start=k == 0, stop=k == KD - 1)
                ins.then_inc(out_ready, 1)

            def rows_T(t):
                r = ROWS[t]
                pe.wait_ge(hn_ready, t + 1)
                for s in range(2):
                    above(pe, hnT_taken[s], t)
                for k in range(KD):
                    ins = transpose(ps[:, 4 + k // 4, (k % 4) * P:(k % 4) * P + r], hn[0:r, t, k * P:(k + 1) * P],
                                    ident[0:r, 0:r])
                ins.then_inc(hnT_ready, 1)

            def route(t):
                r = ROWS[t]
                for s in range(2):
                    pe.wait_ge(hnT_taken[s], t + 1)
                for k in range(KD):
                    ins = mm(ps[0:r, 6, t * 36:(t + 1) * 36], hnT[t % 2][:, k, 0:r], w_route[:, k, :],
                             start=k == 0, stop=k == KD - 1)
                ins.then_inc(logit_ready, 1)

            pe.wait_ge(wo_in, 32)
            pe.wait_ge(route_in, 32)
            pe.wait_ge(merged_ready, 2 * KD)
            for t in range(NT + 1):
                if t < NT:
                    rows_out(t)
                if t > 1:
                    route(t - 2)
                if t > 0:
                    rows_T(t - 1)
            route(NT - 1)
            pe.wait_ge(choice_ready, 1)
            for t in range(NT):
                for j in range(t + 1):
                    mm(ps[:, 7, t * NE:(t + 1) * NE], before_bf if j == t else ones_bf, one_hot_bf[:, j, :],
                       start=j == 0, stop=j == t)
            for t in range(NT):
                ins = mm(ps[:, 7, 256:256 + NE], ones_bf, one_hot_bf[:, t, :], start=t == 0, stop=t == NT - 1)
            ins.then_inc(count_ready, 1)

            def before_transposing(sem, value):
                pe.wait_ge(sem, value)
                pe.sem_inc(passed_pe, 1)

            def turn_x(e, s, full):
                before_transposing(xr_full[s], full)
                rows = x_rows[s][0:C, 0:D].rearrange("c (p j) -> c j p", j=JX)
                for j in range(JX):
                    ins = transpose(ps[:, s, j * C:(j + 1) * C], rows[:, j, :], ident[0:C, 0:C])
                ins.then_inc(xe_ready, 1)

            def gate_up(e, s, ring, full):
                pe.wait_ge(xe_taken, e + 1)
                pe.wait_ge(gu_full[ring], full)
                for j in range(JX):
                    mm(ps[0:C, 2 + s, :], xT[s][:, j, :], w_up[ring][:, j, :], start=j == 0, stop=j == JX - 1)
                    ins = mm(ps[64:64 + C, 2 + s, :], xT[s][:, j, :], w_gate[ring][:, j, :], start=j == 0, stop=j == JX - 1)
                ins.then_inc(gu_ready, 1)

            def turn_hid(e, s):
                before_transposing(hid_ready, e + 1)
                rows = hid[s][0:C, :].rearrange("c (p j) -> c j p", j=JH)
                for j in range(JH):
                    ins = transpose(ps[:, 4 + s, j * C:(j + 1) * C], rows[:, j, :], ident[0:C, 0:C])
                ins.then_inc(hidT_ready, 1)

            def down(e, s, ring, full):
                pe.wait_ge(hidT_taken, e + 1)
                pe.wait_ge(dn_full[ring], full)
                for q in range(2):
                    above(pe, y_taken[q], e - 1)
                for j in range(JH):
                    for q in range(2):
                        ins = mm(ps[64 * q:64 * q + C, 6 + s, :], hidT[s][:, j, :], w_down[ring][:, j, 512 * q:512 * q + 512],
                                 start=j == 0, stop=j == JH - 1)
                ins.then_inc(dn_ready, 1)

            def step(e, k, half, turn, last=False):
                s = k % 2
                if not last:
                    turn_x(e + 1, 1 - s, (half + 1 + s) * 16)
                ring, before = k % NSLOT, (k - 1) % NSLOT
                if not isinstance(e, int) or e > 0:
                    turn_hid(e - 1, 1 - s)
                gate_up(e, s, ring, (turn + 1) * 32)
                if not isinstance(e, int) or e > 0:
                    down(e - 1, 1 - s, before, (turn + 1 - (1 if ring == 0 else 0)) * 16)

            turn_x(0, 0, 16)
            step(0, 0, 0, 0)
            for k in range(1, 1 + UNROLL):
                step(k, k, k // 2, k // NSLOT)
            with pe.Fori(1, STEPS) as it:
                for k in range(1, 1 + UNROLL):
                    step(it * UNROLL + k, k, it * (UNROLL // 2) + k // 2, it * (UNROLL // NSLOT) + k // NSLOT)
            e = NE - 1
            step(e, e, e // 2, e // NSLOT, last=True)
            turn_hid(e, 1)
            down(e, 1, e % NSLOT, 16 * (e // NSLOT + 1))
            filled = -(-NE // NSLOT)
            pe.wait_ge(item_ready, 1)
            n_item = pe.value_load(n_item_i[0:1, 0:1], min_val=0, max_val=NOV)
            with pe.If(n_item > 0):
                with pe.Fori(0, n_item) as i:
                    turn_x(i + NE, 0, i * 16 + 16 * (NE // 2 + 1))
                    gate_up(i + NE, 0, 0, i * 32 + 32 * (filled + 1))
                    turn_hid(i + NE, 0)
                    down(i + NE, 0, 0, i * 16 + 16 * (filled + 1))


def kernel(x_prompt, x_sample, cache_k, cache_v, state_pool, norm_mix_g, w_in, q_norm_g, k_norm_g, attn_sinks,
           w_attn_branch, pool_mix_w, pool_scale, w_pool_branch, w_out, norm_ffn_g, w_route_group,
           b_route_group, w_route_expert, b_route_expert, w_expert_gate, w_expert_up, w_expert_down):
    import concourse.bacc as bacc
    from concourse.bass_utils import run_bass_kernel_spmd

    f = np.asarray
    arrays = {
        "x": np.concatenate([f(x_prompt).reshape(SEQ, D), f(x_sample).reshape(DEC, D)]),
        "cache_k": f(cache_k).reshape(DEC_B, WIN, P), "cache_v": f(cache_v).reshape(DEC_B, WIN, P),
        "state": f(state_pool).reshape(DEC_B, PAST_U, D),
        "g_mix": f(norm_mix_g).reshape(KD, P).T, "w_in": f(w_in)[0], "gq": f(q_norm_g)[0], "gk": f(k_norm_g)[0],
        "sinks": f(attn_sinks)[0],
        "dec_sinks": np.tile(np.repeat(f(attn_sinks)[0], DEC_S), 2).reshape(P, 1),
        "w_attn": f(w_attn_branch)[0], "w_mix": f(pool_mix_w).reshape(D, 256), "p_scale": f(pool_scale).reshape(KD, P).T,
        "w_pool": f(w_pool_branch)[0], "w_out": f(w_out)[0], "g_ffn": f(norm_ffn_g)[0],
        "w_group": f(w_route_group)[0], "b_group": f(b_route_group)[0],
        "w_expert": f(w_route_expert)[0], "b_expert": f(b_route_expert)[0],
        "w_eg": f(w_expert_gate)[0], "w_eu": f(w_expert_up)[0], "w_ed": f(w_expert_down)[0],
        "const": constants(),
    }
    outs = {"y": (T, D), "kp": (WIN, P), "vp": (WIN, P), "up": (PAST_U, D),
            "ks": (DEC_B, WIN, P), "vs": (DEC_B, WIN, P), "us": (DEC_B, PAST_U, D)}
    nc = bacc.Bacc("TRN2", target_bir_lowering=False, num_devices=1)
    a, o = {}, {}
    for name, v in arrays.items():
        arrays[name] = v = np.ascontiguousarray(v)
        a[name] = nc.dram_tensor(f"in_{name}", v.shape, mybir.dt.from_np(v.dtype), kind="ExternalInput").ap()
    for name, shape in outs.items():
        o[name] = nc.dram_tensor(f"out_{name}", shape, F32, kind="ExternalOutput").ap()
    a["w_eg"] = a["w_eg"].rearrange("e (p j) n -> e p j n", j=JX)
    a["w_eu"] = a["w_eu"].rearrange("e (p j) n -> e p j n", j=JX)
    a["w_ed"] = a["w_ed"].rearrange("e (p j) n -> e p j n", j=JH)
    build(nc, a, o)
    r = run_bass_kernel_spmd(nc, [{f"in_{n}": v for n, v in arrays.items()}], core_ids=[0]).results[0]
    got = {n: r[f"out_{n}"] for n in outs}
    kv = (1, -1, WIN, NKV, HD)
    return (got["y"][:SEQ].reshape(1, SEQ, D), got["y"][SEQ:].reshape(DEC_B, DEC_S, D),
            got["kp"].reshape(kv), got["vp"].reshape(kv), got["up"].reshape(1, 1, PAST_U, D),
            got["ks"].reshape(kv), got["vs"].reshape(kv), got["us"].reshape(1, DEC_B, PAST_U, D))
```

```python
from contextlib import ExitStack

import numpy as np

import concourse.bass as bass
from concourse import mybir

ALU = mybir.AluOpType
ACT = mybir.ActivationFunctionType
AX_X = mybir.AxisListType.X
F32 = mybir.dt.float32
BF16 = mybir.dt.bfloat16
U32 = mybir.dt.uint32
I32 = mybir.dt.int32

P = 128
D = 1024
KD = D // P
SEQ = 512
DEC_B, DEC_S = 8, 4
DEC = DEC_B * DEC_S
T = SEQ + DEC
NT = 5
ROWS = [P, P, P, P, DEC]
HALF = T // 2
PAST_LEN = 2048
HD = 64
NKV, NI = 2, 8
NH = NKV * NI
WIN = 128
POOL_W = (2, 4, 8, 16)
PAST_U = 15
KV_OFF, U_OFF, GA_OFF, GP_OFF = 1024, 1280, 2304, 3328
EPS = 1e-6
NG, EG = 4, 8
NE = NG * EG
DE = 512
JX, JH = D // P, DE // P
C = 64
ROWS_SORTED = 2 * T
NOV = (ROWS_SORTED - 1) // C
XW = D + 8
NSLOT = 3
UNROLL = 6
MASKED = -1.0e30

UP = 16
USEG = UP + DEC_S
UW = UP + SEQ + DEC_B * USEG

CONST = {}
_at = 0
for _name, _n in (("ident", 128), ("dec_mask", 4 * 160), ("cos", NT * 32), ("sin", NT * 32),
                  ("inv_count", 4 * 16), ("live", NT), ("group_rank", NG), ("expert_rank", EG),
                  ("expert_id", NE), ("row", 1), ("chunk_edge", 8), ("item", NOV), ("before", P), ("band", 2 * P), ("spare", 1)):
    CONST[_name] = (_at, _n)
    _at += _n
NCONST = _at


def constants():
    c = np.zeros((P, NCONST), np.float32)

    def put(name, value):
        a, n = CONST[name]
        c[:, a:a + n] = np.asarray(value, np.float32).reshape(-1, n)

    put("ident", np.eye(P))
    m = np.full((P, 4, 160), MASKED, np.float32)
    for row in range(P):
        bb, s = row // 64, row % DEC_S
        for g in range(4):
            m[row, g, s + 1:128] = 0
            first = 128 + (2 * g + bb) * DEC_S
            m[row, g, first:first + s + 1] = 0
    put("dec_mask", m.reshape(P, -1))
    pos = np.zeros((P, NT), np.float32)
    for t in range(4):
        pos[:, t] = t * P + np.arange(P)
    pos[:, 4] = PAST_LEN + np.arange(P) % DEC_S
    inv = (np.float32(10000.0) ** (-np.arange(32, dtype=np.float32) * np.float32(2.0 / HD))).astype(np.float32)
    ang = pos[:, :, None] * inv[None, None, :]
    put("cos", np.cos(ang).reshape(P, -1))
    put("sin", np.sin(ang).reshape(P, -1))
    put("inv_count", np.array([[1.0 / min(w, t + 1) for t in range(16)] for w in POOL_W]).reshape(1, -1))
    live = np.ones((P, NT), np.float32)
    live[DEC:, 4] = 0
    put("live", live)
    put("group_rank", NG - np.arange(NG))
    put("expert_rank", EG - np.arange(EG))
    put("expert_id", np.arange(NE))
    put("row", np.arange(P).reshape(P, 1))
    put("chunk_edge", C * (1 + np.arange(8)))
    put("item", np.arange(NOV))
    q, k = np.arange(P)[:, None], np.arange(P)[None, :]
    put("before", q < k)
    put("spare", T + q)
    put("band", np.concatenate([np.where(k > q, 0, MASKED), np.where(k <= q, 0, MASKED)], axis=1))
    return c


def above(eng, sem, value):
    if isinstance(value, int) and value <= 0:
        return
    eng.wait_ge(sem, value)


def build(nc, a, o):
    with ExitStack() as ctx:
        def sb(name, shape, dt=F32):
            return ctx.enter_context(nc.sbuf_tensor(name, shape, dt))

        def sem(name):
            return ctx.enter_context(nc.semaphore(name))

        x = sb("x", [P, NT, D])
        const = sb("const", [P, NCONST])
        cbf = sb("cbf", [P, 3 * P + NKV * 2 * P], BF16)
        g_mix = sb("g_mix", [P, KD])
        p_scale = sb("p_scale", [P, KD])
        sinks = sb("sinks", [P, NKV, NI])
        neg_sink = sb("neg_sink", [P, NI, NKV])
        dec_sink = sb("dec_sink", [P, 2])
        eps = sb("eps", [P, 1])
        r_bias = sb("r_bias", [P, NG + NE])
        w_route = sb("w_route", [P, KD, NG + NE])
        stat = sb("stat", [P, 3, NT])
        z_stat = sb("z_stat", [P, 2, 3, 8])
        a_stat = sb("a_stat", [P, 2, 4, 8])
        d_stat = sb("d_stat", [P, 4, 4])
        kT_pad = sb("kT_pad", [P, NKV, T])
        ARENA = 43648
        arena = sb("arena", [P, ARENA])

        def split(v, shape):
            if len(shape) == 1:
                return v
            names = "abcd"[:len(shape)]
            return v.rearrange(f"p ({' '.join(names)}) -> p {' '.join(names)}", **dict(zip(names, shape)))

        def area(at, *shape):
            n = int(np.prod(shape))
            assert at + n <= ARENA
            return split(arena[:, at:at + n], shape)

        hT = area(0, KD, T)
        attnT = area(4352, KD, T)
        mixedT = area(8704, KD, T)
        w_slot = [13056, 17152]
        pooledT = area(21248, KD, T)
        uT = area(25600, KD, UW)
        qT = area(31104, KD, T)
        mergedT = qT
        WORK = 35456
        xs = [area(31104 + s * D, D) for s in range(2)]
        x_sq = area(31104 + 2 * D, D)
        z_raw = [area(WORK + s * 512, 512) for s in range(2)]
        z_sq = [area(WORK + 1024 + s * 512, 512) for s in range(2)]
        z_norm, z_cos, z_sin = (area(WORK + 2048 + s * 512, 512) for s in range(3))
        q_rows = [area(WORK + 3584 + s * 512, 512) for s in range(2)]
        rot = area(4352, 4, NT, HD)
        g_qk = area(4352 + 4 * NT * HD, 2, HD)
        win_sum = [area(w_slot[1] + 2048 + s * UW, UW) for s in range(2)]
        kc_rows = area(8704, DEC_B, P)
        vc_rows = area(8704 + 3072, DEC_B, P)
        kcT_pad = area(8704 + 1024, DEC_B, NKV, P)
        past_u = area(21248, D)
        probs = [area(WORK + s * 2048, 2048) for s in range(2)]
        probsT = [area(WORK + 4096 + s * 512, 512) for s in range(4)]
        k_rows = area(WORK + 6144, NT, P)
        v_rows = area(WORK + 6784, NT, P)
        q_decT = area(WORK + 7424, DEC_B, NI, DEC_S)
        u_decT = area(WORK + 7680, KD, DEC)
        d_probs = area(WORK, 4, 256)
        new_u = area(WORK + 2048, 2, D)
        gates = [[area(25600 + (2 * h + j) * HALF, HALF) for j in range(2)] for h in range(2)]
        gated = [[area(25600 + (4 + 2 * h + j) * HALF, HALF) for j in range(2)] for h in range(2)]
        w_out = area(WORK, KD, D)
        hn = area(25600, NT, XW)
        hnT = [area(20480 + s * D, KD, P) for s in range(2)]
        g_ffn = area(24576, D)
        RING = [0, 12288, 31104]
        w_up = [area(at, JX, DE) for at in RING]
        w_gate = [area(at + 4096, JX, DE) for at in RING]
        w_down = [area(at + 8192, JH, D) for at in RING]
        EW = 24576
        x_rows = [area(EW + s * XW, XW) for s in range(2)]
        xT = [area(EW + 2 * XW + s * 512, JX, C) for s in range(2)]
        OV = EW + 2 * XW + 1024
        PAD_AT = 30760
        late = x[:].rearrange("p t n -> p (t n)")
        silu = [late[:, s * 512:s * 512 + DE] for s in range(2)]
        hid = [late[:, 1024 + s * 512:1024 + s * 512 + DE] for s in range(2)]
        hidT = [split(late[:, 2048 + s * 256:2048 + (s + 1) * 256], (JH, C)) for s in range(2)]
        y_rows = [late[:, 2560 + s * D:2560 + (s + 1) * D] for s in range(2)]

        one_hot_bf = sb("one_hot_bf", [P, NT, NE], BF16)
        count = sb("count", [P, NE])
        start = sb("start", [P, NE])
        start_i = sb("start_i", [P, NE], I32)
        item = sb("item", [P, 3, NOV])
        item_i = sb("item_i", [P, 2, NOV], I32)
        n_item_i = sb("n_item_i", [P, 1], I32)
        place_i = sb("place_i", [P, NT, 2], U32)
        row_i = [sb(f"row_i{s}", [P, 1], U32) for s in range(2)]
        row_w = [sb(f"row_w{s}", [P, 1]) for s in range(2)]
        row_meta = [sb(f"row_meta{s}", [P, 5]) for s in range(2)]
        row_tmp = sb("row_tmp", [P, 4])

        ps = ctx.enter_context(nc.psum_tensor("ps", [P, 8, 512], F32))

        def cc(name, *shape):
            at, n = CONST[name]
            return split(const[:, at:at + n], shape or (n,))

        ident = cc("ident")
        ident_bf, before_bf, ones_bf = (cbf[:, n * P:(n + 1) * P] for n in range(3))
        band = cbf[:, 3 * P:].rearrange("p (v k) -> p v k", v=NKV)

        sorted_rows = nc.dram_tensor("sorted_rows", (ROWS_SORTED + C, XW), F32, kind="Internal").ap()

        ident_in = sem("ident_in")
        const_in = sem("const_in")
        route_in = sem("route_in")
        gffn_in = sem("gffn_in")
        x_in = [sem(f"x_in{t}") for t in range(NT)]
        cache_in = sem("cache_in")
        state_in = sem("state_in")
        w_full = [sem(f"w_full{s}") for s in range(2)]
        w_used = sem("w_used")
        zeros_set = sem("zeros_set")
        act_own = sem("act_own")
        dve_own = sem("dve_own")
        pool_own = sem("pool_own")
        ssq_ready = sem("ssq_ready")
        root_ready = sem("root_ready")
        xs_ready = sem("xs_ready")
        xsT_ready = sem("xsT_ready")
        hT_ready = sem("hT_ready")
        z_ready = sem("z_ready")
        z_sq_ready = sem("z_sq_ready")
        z_taken = sem("z_taken")
        z_sum_ready = sem("z_sum_ready")
        z_root_ready = sem("z_root_ready")
        rot_ready = sem("rot_ready")
        rotT_ready = sem("rotT_ready")
        rotT_taken = sem("rotT_taken")
        pastT_ready = sem("pastT_ready")
        pastT_taken = sem("pastT_taken")
        kcT_ready = sem("kcT_ready")
        kcT_taken = sem("kcT_taken")
        u_ready = sem("u_ready")
        u_taken = sem("u_taken")
        pooled_ready = sem("pooled_ready")
        s_ready = sem("s_ready")
        nmax_ready = sem("nmax_ready")
        exp_ready = sem("exp_ready")
        p_ready = sem("p_ready")
        pT_ready = sem("pT_ready")
        pT_taken = [sem("pT_taken_dve"), sem("pT_taken_act")]
        o_ready = sem("o_ready")
        o_taken = sem("o_taken")
        nu_ready = sem("nu_ready")
        nu_taken = sem("nu_taken")
        mix_ready = sem("mix_ready")
        mix_taken = sem("mix_taken")
        gates_ready = sem("gates_ready")
        branch_ready = sem("branch_ready")
        sig_ready = sem("sig_ready")
        gated_own = sem("gated_own")
        merged_ready = sem("merged_ready")
        wo_in = sem("wo_in")
        out_ready = sem("out_ready")
        x2_ready = sem("x2_ready")
        ssq2_ready = sem("ssq2_ready")
        root2_ready = sem("root2_ready")
        hn_ready = sem("hn_ready")
        hnT_ready = sem("hnT_ready")
        hnT_taken = [sem("hnT_taken_dve"), sem("hnT_taken_act")]
        logit_ready = sem("logit_ready")
        diff_ready = sem("diff_ready")
        gexp_ready = sem("gexp_ready")
        choice_ready = sem("choice_ready")
        count_ready = sem("count_ready")
        place_ready = sem("place_ready")
        pad_out = sem("pad_out")
        sorted_out = sem("sorted_out")
        item_ready = sem("item_ready")
        gu_full = [sem(f"gu_full{s}") for s in range(NSLOT)]
        dn_full = [sem(f"dn_full{s}") for s in range(NSLOT)]
        xr_full = [sem(f"xr_full{s}") for s in range(2)]
        xe_ready = sem("xe_ready")
        xe_taken = sem("xe_taken")
        gu_ready = sem("gu_ready")
        silu_ready = sem("silu_ready")
        hid_ready = sem("hid_ready")
        hidT_ready = sem("hidT_ready")
        hidT_taken = sem("hidT_taken")
        dn_ready = sem("dn_ready")
        y_taken = [sem("y_taken_dve"), sem("y_taken_act")]
        row_own = sem("row_own")
        row_i_ready = sem("row_i_ready")
        y_out = [sem(f"y_out{s}") for s in range(2)]
        passed_pe, passed_pool, passed_sp = (sem(f"passed_{e}") for e in ("pe", "pool", "sp"))
        kv_out = sem("kv_out")
        nu_out = sem("nu_out")
        spare_out = sem("spare_out")
        y_start = [sem("y_start_first"), sem("y_start_rest")]

        MIX_EARLY = 2
        N_CONST = 7
        w_in = a["w_in"]
        STEPS = (NE - 2) // UNROLL

        def y_written(s, n):
            return n * 16 + 16 * s

        def slot(n, *shape):
            return area(w_slot[n % 2], *shape)

        def head_groups():
            for n in range(8):
                b, g = n // 2, n % 2
                yield n, b, 4 * g, (P if b == 0 else 2 * P), ([0] if b == 0 else [b - 1, b])

        turns = [(n, kb, v) for n, b, g, w, tiles in head_groups() for kb in range(len(tiles)) for v in range(NKV)]
        first_turn = [next(k for k, tn in enumerate(turns) if tn[0] == n) for n in range(8)] + [len(turns)]
        assert len(turns) % 2 == 0

        def take_probsT(eng, copy, k):
            eng.wait_ge(pT_ready, k + 1)
            n = turns[k][0] if k < len(turns) else 8 + k - len(turns)
            above(eng, o_ready, n)
            w = 512 if k < len(turns) else 256
            copy(probsT[k % 4][:, 0:w], ps[:, 4 + k % 2, 0:w]).then_inc(pT_taken[k % 2], 1)

        def scratch():
            at = [0]

            def take(*shape):
                n = int(np.prod(shape))
                at[0] += n
                assert at[0] <= 2 * D
                return split(late[:, at[0] - n:at[0]], shape)
            return take

        take = scratch()
        logits = take(NT, NG + NE)
        g_diff, g_exp = take(NT, NG), take(NT, NG)
        e_diff, e_exp = take(NT), take(NT)
        route_exp = [(g_diff, g_exp), (e_diff, e_exp)]
        g_hot, g_tmp = take(NT, NG), take(NT, NG)
        picked, e_tmp, e_hot1, e_hot2 = (take(NT, EG) for _ in range(4))
        wide, hot1, hot2 = (take(NT, NE) for _ in range(3))
        vec = [take(NT) for _ in range(6)]
        cum = [take(2 * NE) for _ in range(2)]

        block = ctx.enter_context(nc.Block())

        @block.sync
        def _(sp):
            def k_major(v):
                return v.rearrange("(k p) n -> p k n", p=P)

            sp.dma_start(x[:, 0, :], a["x"][0:P, :]).then_inc(x_in[0], 16)
            sp.dma_start(const[:], a["const"]).then_inc(ident_in, 16)
            sp.dma_start(g_mix[:], a["g_mix"]).then_inc(ident_in, 16)
            for t in range(1, NT):
                sp.dma_start(x[0:ROWS[t], t, :], a["x"][t * P:t * P + ROWS[t], :]).then_inc(x_in[t], 16)
            sp.dma_start(slot(0, KD, 256), k_major(w_in[:, KV_OFF:U_OFF])).then_inc(w_full[0], 16)
            sp.dma_start(p_scale[:], a["p_scale"]).then_inc(const_in, 16)
            sp.dma_start(g_qk[:, 0, :], a["gq"].partition_broadcast(P)).then_inc(const_in, 16)
            sp.dma_start(g_qk[:, 1, :], a["gk"].partition_broadcast(P)).then_inc(const_in, 16)
            sp.dma_start(sinks[:].rearrange("p v i -> p (v i)"), a["sinks"].partition_broadcast(P)).then_inc(const_in, 16)
            sp.dma_start(dec_sink[:, 0:1], a["dec_sinks"]).then_inc(const_in, 16)
            sp.dma_start(r_bias[:, 0:NG], a["b_group"].partition_broadcast(P)).then_inc(const_in, 16)
            sp.dma_start(r_bias[:, NG:], a["b_expert"].partition_broadcast(P)).then_inc(const_in, 16)
            for g in range(2):
                if g == 1:
                    sp.wait_ge(w_used, 1)
                dst = slot(1 + g, KD, NKV, 256)
                for v in range(NKV):
                    at = v * 512 + g * 256
                    sp.dma_start(dst[:, :, v, :], k_major(w_in[:, at:at + 256])).then_inc(w_full[(1 + g) % 2], 16)
            sp.dma_start(w_route[:, :, 0:NG], k_major(a["w_group"])).then_inc(route_in, 16)
            sp.dma_start(w_route[:, :, NG:], k_major(a["w_expert"])).then_inc(route_in, 16)
            sp.dma_start(past_u[0:DEC_B * PAST_U, :], a["state"].rearrange("b s c -> (b s) c")).then_inc(state_in, 16)
            sp.dma_start(kc_rows, a["cache_k"].rearrange("b w c -> w b c")).then_inc(cache_in, 16)
            sp.dma_start(vc_rows, a["cache_v"].rearrange("b w c -> w b c")).then_inc(cache_in, 16)
            for n in range(3, 5):
                sp.wait_ge(w_used, n - 1)
                at = U_OFF + 512 * (n - 3)
                sp.dma_start(slot(n, KD, 512), k_major(w_in[:, at:at + 512])).then_inc(w_full[n % 2], 16)
            sp.wait_ge(w_used, 4)
            sp.dma_start(slot(5, KD, 256), k_major(a["w_mix"])).then_inc(w_full[1], 16)

            def load_merge(m, s):
                cols = bass.ts(m, P)
                dst = area(w_slot[s], 4, KD, P)
                for j, off in ((0, GA_OFF), (1, GP_OFF)):
                    sp.dma_start(dst[:, j], k_major(w_in[:, off:off + D])[:, :, cols]).then_inc(w_full[s], 16)
                att = a["w_attn"].rearrange("(v i d) n -> v d i n", v=NKV, i=NI)
                for v in range(NKV):
                    sp.dma_start(dst[64 * v:64 * v + 64, 2], att[v][:, :, cols]).then_inc(w_full[s], 16)
                sp.dma_start(dst[:, 3], k_major(a["w_pool"])[:, :, cols]).then_inc(w_full[s], 16)

            sp.wait_ge(w_used, 5)
            load_merge(0, 0)
            sp.wait_ge(w_used, 6)
            load_merge(1, 1)
            sp.wait_ge(o_taken, 12)
            sp.wait_ge(kv_out, 16 * 6)
            sp.wait_ge(nu_out, 16 * 3)
            for kk in range(2):
                sp.dma_start(w_out[:, 4 * kk:4 * kk + 4, :], k_major(a["w_out"])[:, 4 * kk:4 * kk + 4, :])\
                  .then_inc(wo_in, 16)
            with sp.Fori(0, KD // 2 - 1) as it:
                for s in range(2):
                    m = it * 2 + s
                    sp.wait_ge(branch_ready, m * 2 + 2)
                    load_merge(m + 2, s)

            def load_gu(e, s):
                sp.dma_start(w_up[s], a["w_eu"][bass.ds(e, 1)].squeeze(0)).then_inc(gu_full[s], 16)
                sp.dma_start(w_gate[s], a["w_eg"][bass.ds(e, 1)].squeeze(0)).then_inc(gu_full[s], 16)

            def load_down(e, s):
                sp.dma_start(w_down[s], a["w_ed"][bass.ds(e, 1)].squeeze(0)).then_inc(dn_full[s], 16)

            def load_x(first, s):
                sp.dma_start(x_rows[s][0:C, :], sorted_rows[bass.ds(first, C), :]).then_inc(xr_full[s], 16)

            sp.wait_ge(branch_ready, 2 * KD)
            sp.dma_start(g_ffn, a["g_ffn"].partition_broadcast(P)).then_inc(gffn_in, 16)
            load_gu(0, 0)
            load_down(0, 0)
            load_gu(1, 1)
            for t in range(NT):
                sp.wait_ge(x2_ready, t + 1)
                sp.dma_start(o["y"][t * P:t * P + ROWS[t], :], x[0:ROWS[t], t, :]).then_inc(y_start[0 if t < 2 else 1], 16)
            load_gu(2, 2)
            load_down(2, 2)
            sp.wait_ge(logit_ready, NT)
            load_down(1, 1)
            sp.wait_ge(sorted_out, 16 * 2 * NT)
            sp.wait_ge(pad_out, 32)
            for e in range(3):
                if e > 1:
                    sp.wait_ge(xe_taken, 1)
                load_x(sp.value_load(start_i[0:1, e:e + 1], min_val=0, max_val=ROWS_SORTED), e % 2)

            def follow(e, k, rows_left=True):
                sp.wait_ge(gu_ready, e + 1)
                sp.sem_inc(passed_sp, 1)
                if rows_left:
                    sp.wait_ge(xe_taken, e + 2)
                    sp.sem_inc(passed_sp, 1)
                    first = sp.value_load(start_i[0:1, bass.ds(e + 3, 1)], min_val=0, max_val=ROWS_SORTED)
                    load_x(first, (k + 1) % 2)
                load_gu(e + NSLOT, k % NSLOT)
                sp.wait_ge(dn_ready, e + 1)
                load_down(e + NSLOT, k % NSLOT)

            bodies = (NE - NSLOT) // UNROLL
            with sp.Fori(0, bodies) as it:
                for k in range(UNROLL):
                    follow(it * UNROLL + k, k)
            for e in range(bodies * UNROLL, NE - NSLOT):
                follow(e, e - bodies * UNROLL, rows_left=e + 3 < NE)

            sp.wait_ge(item_ready, 1)
            sp.wait_ge(dn_ready, NE)
            n_item = sp.value_load(n_item_i[0:1, 0:1], min_val=0, max_val=NOV)
            with sp.If(n_item > 0):
                with sp.Fori(0, n_item) as i:
                    expert = sp.value_load(item_i[0:1, 0, bass.ds(i, 1)], min_val=0, max_val=NE - 1)
                    first = sp.value_load(item_i[0:1, 1, bass.ds(i, 1)], min_val=0, max_val=ROWS_SORTED)
                    load_x(first, 0)
                    load_gu(expert, 0)
                    load_down(expert, 0)
                    sp.wait_ge(y_out[0], i * 16 + 16 * (NE // 2 + 1))
                    sp.sem_inc(passed_sp, 1)

            for s in range(2):
                sp.wait_ge(y_out[s], y_written(s, NE // 2))

        @block.gpsimd
        def _(pool):
            pool.memset(eps[:], EPS).then_inc(zeros_set, 1)
            pool.memset(kT_pad[:], 0.0).then_inc(zeros_set, 1)
            pool.memset(kcT_pad, 0.0).then_inc(zeros_set, 1)
            pool.memset(uT[:, :, 0:UP], 0.0).then_inc(zeros_set, 1)
            for m in range(KD):
                pool.memset(split(uT[:, m, UP + SEQ:], (DEC_B, USEG))[:, :, 0:1], 0.0).then_inc(zeros_set, 1)
            for q in range(1, 4):
                pool.wait_ge(zeros_set, KD + 3 + q)
                pool.memset(v_rows[32 * q:32 * q + 32, 4, :], 0.0).then_inc(zeros_set, 1)
            pool.wait_ge(zeros_set, KD + 7)
            pool.dma_start(o["ks"][:, 0:WIN - DEC_S, :], a["cache_k"][:, DEC_S:, :]).then_inc(kv_out, 16)
            pool.dma_start(o["vs"][:, 0:WIN - DEC_S, :], a["cache_v"][:, DEC_S:, :]).then_inc(kv_out, 16)
            pool.dma_start(o["us"][:, 0:PAST_U - DEC_S, :], a["state"][:, DEC_S:, :]).then_inc(nu_out, 16)
            pool.wait_ge(rot_ready, NT)
            pool.wait_ge(z_taken, NT)
            pool.dma_start(o["kp"], k_rows[:, 3, :]).then_inc(kv_out, 16)
            pool.dma_start(o["vp"], v_rows[:, 3, :]).then_inc(kv_out, 16)
            pool.dma_start(o["ks"][:, WIN - DEC_S:, :], k_rows[0:DEC, 4, :]).then_inc(kv_out, 16)
            pool.dma_start(o["vs"][:, WIN - DEC_S:, :], v_rows[0:DEC, 4, :]).then_inc(kv_out, 16)
            pool.wait_ge(nu_taken, 2)
            pool.dma_start(o["up"], new_u[0:PAST_U, 0, :]).then_inc(nu_out, 16)
            pool.dma_start(o["us"][:, PAST_U - DEC_S:, :], new_u[0:DEC, 1, :]).then_inc(nu_out, 16)
            pool.wait_ge(nu_out, 48)
            pad = area(PAD_AT, XW // 4)
            pool.memset(pad, 0.0).then_inc(pool_own, 1)
            pool.wait_ge(pool_own, 1)
            quarters = sorted_rows[ROWS_SORTED:, :].rearrange("c (q n) -> (c q) n", q=4)
            for h in range(2):
                pool.dma_start(quarters[h * P:(h + 1) * P, :], pad).then_inc(pad_out, 16)
            spare = o["y"][T:, :].rearrange("c (q n) -> (c q) n", q=4)
            for h, zeroed in enumerate((spare_out, y_out[1])):
                pool.dma_start(spare[h * P:(h + 1) * P, :], pad[:, 0:D // 4]).then_inc(zeroed, 16)
            pool.wait_ge(place_ready, 1)
            for t in range(NT):
                r = ROWS[t]
                for c in range(2):
                    pool.indirect_dma_start(
                        out=sorted_rows, out_offset=bass.IndirectOffsetOnAxis(ap=place_i[0:r, t, c:c + 1], axis=0),
                        in_=hn[0:r, t, :], in_offset=None).then_inc(sorted_out, 16)

            def put_y(e, s, others):
                pool.wait_ge(y_taken[0], e + 1)
                pool.wait_ge(y_taken[1], e + 1)
                pool.wait_ge(row_i_ready, e + 1)
                pool.wait_ge(y_out[1 - s], y_written(1 - s, others))
                pool.sem_inc(passed_pool, 1)
                pool.indirect_dma_start(
                    out=o["y"], out_offset=bass.IndirectOffsetOnAxis(ap=row_i[s][0:C, :], axis=0),
                    in_=y_rows[s][0:C, :], in_offset=None, compute_op=ALU.add).then_inc(y_out[s], 16)

            pool.wait_ge(y_start[0], 32)
            pool.wait_ge(y_start[1], 16 * (NT - 2))
            pool.wait_ge(spare_out, 16)
            with pool.Fori(0, NE // 2) as it:
                for s in range(2):
                    put_y(it * 2 + s, s, it + s)
            pool.wait_ge(item_ready, 1)
            n_item = pool.value_load(n_item_i[0:1, 0:1], min_val=0, max_val=NOV)
            with pool.If(n_item > 0):
                with pool.Fori(0, n_item) as i:
                    put_y(i + NE, 0, NE // 2)

        @block.scalar
        def _(act):
            def copy(out, in_):
                return act.activation(out, in_, ACT.Copy)

            act.wait_ge(zeros_set, 1)
            for t in range(NT):
                r = ROWS[t]
                act.wait_ge(x_in[t], 16)
                act.activation(x_sq[0:r, :], x[0:r, t, :], ACT.Square, accum_out=stat[0:r, 0, t:t + 1])\
                   .then_inc(ssq_ready, 1)
                act.wait_ge(ssq_ready, t + 1)
                act.activation(stat[0:r, 1, t:t + 1], stat[0:r, 0, t:t + 1], ACT.Sqrt, bias=eps[0:r, :],
                               scale=1.0 / D).then_inc(root_ready, 1)

            act.wait_ge(zeros_set, 3 + KD + 4)
            for n in range(3 * NT):
                u, t = n // NT, n % NT
                r, s, bank = ROWS[t], n % 2, 4 + n % 4
                w = P if u == 0 else 512
                act.wait_ge(z_ready, n + 1)
                above(act, rot_ready, n - 1)
                parts = 4 if t == NT - 1 and u > 0 else 1
                m = w // parts
                for q in range(parts):
                    ins = act.activation(z_sq[s][0:r, q * m:(q + 1) * m], ps[q * r:(q + 1) * r, bank, 0:m], ACT.Square)
                ins.then_inc(z_sq_ready, 1)
                if u == 0:
                    copy(v_rows[0:r, t, :], ps[0:r, bank, P:2 * P])
                for q in range(parts):
                    ins = copy(z_raw[s][0:r, q * m:(q + 1) * m], ps[q * r:(q + 1) * r, bank, 0:m])
                ins.then_inc(z_taken, 1)
                act.wait_ge(z_sum_ready, n + 1)
                act.activation(z_stat[0:r, s, 1, 0:w // HD], z_stat[0:r, s, 0, 0:w // HD], ACT.Sqrt,
                               bias=eps[0:r, :], scale=1.0 / HD).then_inc(z_root_ready, 1)

            def take_u(m, h):
                act.wait_ge(u_ready, 2 * m + h + 1)
                if h == 0:
                    copy(uT[:, m, UP:UP + HALF], ps[:, 7, 0:HALF]).then_inc(u_taken, 1)
                    return
                copy(uT[:, m, UP + HALF:UP + SEQ], ps[:, 7, 0:SEQ - HALF])
                copy(u_decT[:, m, :], ps[:, 7, SEQ - HALF:HALF])
                copy(split(uT[:, m, UP + SEQ:], (DEC_B, USEG))[:, :, UP:],
                     split(ps[:, 7, SEQ - HALF:HALF], (DEC_B, DEC_S))).then_inc(u_taken, 1)

            def exponentials(n, w):
                act.wait_ge(nmax_ready, n + 1)
                s = n % 2
                pb = split(probs[s][:, 0:8 * w], (4, NKV, w))
                for i in range(4):
                    for v in range(NKV):
                        c = i * NKV + v
                        act.activation(pb[:, i, v, :], ps[:, i, v * w:(v + 1) * w], ACT.Exp,
                                       bias=a_stat[:, s, 0, c:c + 1], accum_out=a_stat[:, s, 1, c:c + 1])
                act.activation(a_stat[:, s, 3, :], a_stat[:, s, 2, :], ACT.Exp).then_inc(exp_ready, 1)

            groups = list(head_groups())
            exponentials(0, P)
            for n, b, i0, w, tiles in groups:
                take_u(n, 0)
                for k in range(first_turn[n], first_turn[n + 1]):
                    if k % 2 == 1:
                        take_probsT(act, copy, k)
                take_u(n, 1)
                if n < 7:
                    exponentials(n + 1, groups[n + 1][3])
                act.wait_ge(o_ready, n + 1)
                copy(attnT[:, i0:i0 + 4, b * P:(b + 1) * P], split(ps[:, 6, :], (4, P))).then_inc(o_taken, 1)

            def take_mix(m):
                act.wait_ge(mix_ready, m + 1)
                for h in range(2):
                    ins = act.activation(mixedT[:, m, h * HALF:(h + 1) * HALF],
                                         ps[:, 4 + 2 * (m % 2) + h, 0:HALF], ACT.Copy, scale=p_scale[:, m:m + 1])
                ins.then_inc(mix_taken, 1)

            act.wait_ge(nmax_ready, 9)
            for g in range(4):
                act.activation(d_probs[:, g, 0:160], d_probs[:, g, 0:160], ACT.Exp, bias=d_stat[:, 0, g:g + 1],
                               accum_out=d_stat[:, 1, g:g + 1])
            act.activation(d_stat[:, 3, :], d_stat[:, 2, :], ACT.Exp).then_inc(exp_ready, 1)
            for m in range(MIX_EARLY):
                take_mix(m)
            for g in range(4):
                if g % 2 == 1:
                    take_probsT(act, copy, len(turns) + g)
                act.wait_ge(o_ready, 9 + g)
                for bb in range(2):
                    at = SEQ + (2 * g + bb) * DEC_S
                    ins = copy(attnT[:, :, at:at + DEC_S],
                               split(ps[:, 6 + g % 2, 32 * bb:32 * bb + 32], (NI, DEC_S)))
                ins.then_inc(o_taken, 1)
            for m in range(MIX_EARLY, KD):
                take_mix(m)

            def sigmoids(q, h, first=False):
                act.wait_ge(gates_ready, q + 1)
                if not first:
                    act.wait_ge(merged_ready, q - 1)
                for j in range(2):
                    ins = act.activation(gates[h][j], ps[:, 4 * h + j, 0:HALF], ACT.Sigmoid)
                ins.then_inc(sig_ready, 1)

            for h in range(2):
                sigmoids(h, h, first=True)
            with act.Fori(1, KD) as m:
                for h in range(2):
                    sigmoids(m * 2 + h, h)

            def take_hnT(t):
                act.wait_ge(hnT_ready, t + 1)
                above(act, logit_ready, t - 1)
                r = ROWS[t]
                copy(hnT[t % 2][:, 4:8, 0:r], split(ps[:, 5, :], (4, P))[:, :, 0:r]).then_inc(hnT_taken[1], 1)

            for t in range(NT):
                r = ROWS[t]
                act.wait_ge(x2_ready, t + 1)
                act.activation(hn[0:r, t, 0:D], x[0:r, t, :], ACT.Square, accum_out=stat[0:r, 0, t:t + 1])\
                   .then_inc(ssq2_ready, 1)
                act.wait_ge(ssq2_ready, t + 1)
                act.activation(stat[0:r, 1, t:t + 1], stat[0:r, 0, t:t + 1], ACT.Sqrt, bias=eps[0:r, :],
                               scale=1.0 / D).then_inc(root2_ready, 1)
                if t:
                    take_hnT(t - 1)
            take_hnT(NT - 1)
            for n in range(2):
                act.wait_ge(diff_ready, n + 1)
                t_in, t_out = route_exp[n]
                act.activation(t_out, t_in, ACT.Exp).then_inc(gexp_ready, 1)

            def take_hidT(e, s):
                act.wait_ge(hidT_ready, e + 1)
                copy(hidT[s], split(ps[:, 4 + s, 0:JH * C], (JH, C))).then_inc(hidT_taken, 1)

            def do_silu(e, s):
                act.wait_ge(gu_ready, e + 1)
                act.activation(silu[s][0:C, :], ps[64:64 + C, 2 + s, :], ACT.Silu).then_inc(silu_ready, 1)

            def take_y(e, s, before):
                act.wait_ge(dn_ready, e + 1)
                above(act, y_out[s], y_written(s, before))
                copy(y_rows[s][0:C, 512:1024], ps[64:64 + C, 6 + s, :]).then_inc(y_taken[1], 1)

            def step(e, k, half):
                s = k % 2
                take_hidT(e - 1, 1 - s)
                do_silu(e, s)
                take_y(e - 1, 1 - s, half - (1 - s))

            act.wait_ge(y_start[0], 32)
            act.wait_ge(y_start[1], 16 * (NT - 2))
            do_silu(0, 0)
            for k in range(1, 1 + UNROLL):
                step(k, k, k // 2)
            with act.Fori(1, STEPS) as it:
                for k in range(1, 1 + UNROLL):
                    step(it * UNROLL + k, k, it * (UNROLL // 2) + k // 2)
            step(NE - 1, 1, (NE - 1) // 2)
            take_hidT(NE - 1, 1)
            take_y(NE - 1, 1, NE // 2 - 1)
            act.wait_ge(item_ready, 1)
            n_item = act.value_load(n_item_i[0:1, 0:1], min_val=0, max_val=NOV)
            with act.If(n_item > 0):
                with act.Fori(0, n_item) as i:
                    do_silu(i + NE, 0)
                    take_hidT(i + NE, 0)
                    take_y(i + NE, 0, i + NE // 2)

        @block.vector
        def _(dve):
            own = [0]

            def link(ins):
                own[0] += 1
                ins.then_inc(dve_own, 1)
                dve.wait_ge(dve_own, own[0])

            def over(v, n):
                return v.unsqueeze(2).to_broadcast((v.shape[0], v.shape[1], n))

            def across(v, n):
                return v.unsqueeze(1).to_broadcast((v.shape[0], n, v.shape[1]))

            tt, ts, stt = dve.tensor_tensor, dve.tensor_scalar, dve.scalar_tensor_tensor
            dve.wait_ge(ident_in, 32)
            for t in range(NT + 1):
                if t < NT:
                    r = ROWS[t]
                    dve.wait_ge(root_ready, t + 1)
                    above(dve, xsT_ready, t - 1)
                    link(dve.reciprocal(stat[0:r, 2, t:t + 1], stat[0:r, 1, t:t + 1]))
                    ts(xs[t % 2][0:r, :], x[0:r, t, :], stat[0:r, 2, t:t + 1], None, ALU.mult).then_inc(xs_ready, 1)
                if t > 0:
                    r, at = ROWS[t - 1], (t - 1) * P
                    dve.wait_ge(xsT_ready, t)
                    for kk in range(2):
                        ins = tt(hT[:, 4 * kk:4 * kk + 4, at:at + r],
                                 split(ps[:, 2 * ((t - 1) % 2) + kk, :], (4, P))[:, :, 0:r],
                                 over(g_mix[:, 4 * kk:4 * kk + 4], r), ALU.mult)
                    ins.then_inc(hT_ready, 1)

            dve.wait_ge(const_in, 16 * N_CONST)
            dve.wait_ge(zeros_set, 3 + KD + 4)
            for c in range(2):
                g = g_qk[:, c, :]
                for half in range(2):
                    own_half, other = slice(32 * half, 32 * half + 32), slice(32 - 32 * half, 64 - 32 * half)
                    tt(rot[:, 2 * c, :, own_half], cc("cos", NT, 32), across(g[:, own_half], NT), ALU.mult)
                    link(tt(rot[:, 2 * c + 1, :, own_half], cc("sin", NT, 32), across(g[:, other], NT), ALU.mult))
                link(ts(rot[:, 2 * c + 1, :, 0:32], rot[:, 2 * c + 1, :, 0:32], -1.0, None, ALU.mult))
            dve.tensor_copy(ident_bf, ident)
            dve.tensor_copy(before_bf, cc("before"))
            dve.memset(ones_bf, 1.0)
            for v in range(NKV):
                ins = dve.tensor_copy(band[:, v, :], cc("band"))
            link(ins)
            link(ts(neg_sink[:].rearrange("p i v -> p v i"), sinks[:], -1.0, None, ALU.mult))
            link(ts(dec_sink[:, 1:2], dec_sink[:, 0:1], -1.0, None, ALU.mult))

            def take_rotT(n):
                u, t = n // NT, n % NT
                r, at = ROWS[t], t * P
                dve.wait_ge(rotT_ready, n + 1)
                if u == 0:
                    for v in range(NKV):
                        rows = slice(64 * v, 64 * v + 64)
                        ins = dve.tensor_copy(kT_pad[rows, v, at:at + r], ps[rows, n % 2, 0:r])
                elif t < NT - 1:
                    ins = ts(qT[:, 4 * (u - 1):4 * u, at:at + r], split(ps[:, n % 2, :], (4, P)),
                             float(HD) ** -0.5, None, ALU.mult)
                else:
                    for i in range(4):
                        ins = ts(q_decT[:, :, 4 * (u - 1) + i, :], split(ps[:, n % 2, i * P:i * P + r], (DEC_B, DEC_S)),
                                 float(HD) ** -0.5, None, ALU.mult)
                ins.then_inc(rotT_taken, 1)

            for n in range(3 * NT):
                u, t = n // NT, n % NT
                r, s = ROWS[t], n % 2
                heads = 2 if u == 0 else 8
                w = heads * HD
                raw, norm, own_part, other_part = (split(v[0:r, 0:w], (heads, HD)) for v in
                                                   (z_raw[s], z_norm, z_cos, z_sin))
                tables = [across(rot[0:r, (2 if u == 0 else 0) + c, t, :], heads) for c in range(2)]
                dve.wait_ge(z_sq_ready, n + 1)
                dve.tensor_reduce(z_stat[0:r, s, 0, 0:heads], split(z_sq[s][0:r, 0:w], (heads, HD)), AX_X, ALU.add)\
                   .then_inc(z_sum_ready, 1)
                dve.wait_ge(z_root_ready, n + 1)
                dve.wait_ge(z_taken, n + 1)
                link(dve.reciprocal(z_stat[0:r, s, 2, 0:heads], z_stat[0:r, s, 1, 0:heads]))
                link(tt(norm, raw, over(z_stat[0:r, s, 2, 0:heads], HD), ALU.mult))
                tt(own_part, norm, tables[0], ALU.mult)
                tt(other_part[:, :, 0:32], norm[:, :, 32:64], tables[1][:, :, 0:32], ALU.mult)
                link(tt(other_part[:, :, 32:64], norm[:, :, 0:32], tables[1][:, :, 32:64], ALU.mult))
                above(dve, rotT_ready, n - 1)
                if u == 0:
                    ins = tt(split(k_rows[0:r, t, :], (heads, HD)), own_part, other_part, ALU.add)
                else:
                    out = split(q_rows[s][0:r, :], (4, NKV, HD)).rearrange("p i v d -> p v i d")
                    ins = tt(out, split(z_cos[0:r, :], (NKV, 4, HD)), split(z_sin[0:r, :], (NKV, 4, HD)), ALU.add)
                ins.then_inc(rot_ready, 1)
                if n:
                    take_rotT(n - 1)
            take_rotT(3 * NT - 1)

            dve.wait_ge(pastT_ready, 1)
            for m in range(KD):
                ins = dve.tensor_copy(split(uT[:, m, UP + SEQ:], (DEC_B, USEG))[:, :, 1:UP],
                                      split(ps[:, 2 + m // 4, (m % 4) * P:(m % 4) * P + DEC_B * PAST_U], (DEC_B, PAST_U)))
            ins.then_inc(pastT_taken, 1)
            dve.wait_ge(kcT_ready, 1)
            for kk in range(2):
                for v in range(NKV):
                    rows = slice(64 * v, 64 * v + 64)
                    ins = dve.tensor_copy(kcT_pad[rows, 4 * kk:4 * kk + 4, v, :], split(ps[rows, 4 + kk, :], (4, P)))
            ins.then_inc(kcT_taken, 1)

            def pool_block(m):
                g = m // 2
                width = POOL_W[g]
                dve.wait_ge(u_taken, 2 * m + 2)
                u = uT[:, m, :]
                src, n = u, 1
                for lvl in range(g + 1):
                    dst = win_sum[lvl % 2]
                    link(tt(dst[:, 2 * n - 1:], src[:, 2 * n - 1:], src[:, n - 1:UW - n], ALU.add))
                    src, n = dst, 2 * n
                out = pooledT[:, m, :]
                link(stt(out[:, 0:SEQ], src[:, UP:UP + SEQ], 1.0 / width, u[:, UP:UP + SEQ], ALU.mult, ALU.subtract))
                dec_sum, dec_u = (split(v[:, UP + SEQ:], (DEC_B, USEG))[:, :, UP:] for v in (src, u))
                stt(split(out[:, SEQ:], (DEC_B, DEC_S)), dec_sum, 1.0 / width, dec_u, ALU.mult, ALU.subtract)
                link(tt(out[:, 0:16], src[:, UP:UP + 16], cc("inv_count", 4, 16)[:, g, :], ALU.mult))
                tt(out[:, 0:16], out[:, 0:16], u[:, UP:UP + 16], ALU.subtract).then_inc(pooled_ready, 1)

            def maxima(n, i0, w):
                s = n % 2
                dve.wait_ge(s_ready, n + 1)
                link(dve.tensor_reduce(split(a_stat[:, s, 0, :], (4, NKV)), ps[:, 0:4, 0:2 * w].rearrange("p i (v k) -> p i v k", v=NKV),
                                       AX_X, ALU.max, negate=True))
                ns = neg_sink[:, i0:i0 + 4, :].rearrange("p i v -> p (i v)")
                link(tt(a_stat[:, s, 0, :], a_stat[:, s, 0, :], ns, ALU.min))
                tt(a_stat[:, s, 2, :], a_stat[:, s, 0, :], ns, ALU.subtract).then_inc(nmax_ready, 1)

            def normalise(n, w):
                s = n % 2
                dve.wait_ge(exp_ready, n + 1)
                link(tt(a_stat[:, s, 1, :], a_stat[:, s, 1, :], a_stat[:, s, 3, :], ALU.add))
                link(dve.reciprocal(a_stat[:, s, 1, :], a_stat[:, s, 1, :]))
                for c in range(8):
                    v = probs[s][:, c * w:(c + 1) * w]
                    ins = ts(v, v, a_stat[:, s, 1, c:c + 1], None, ALU.mult)
                ins.then_inc(p_ready, 1)

            groups = list(head_groups())
            maxima(0, 0, P)
            for n, b, i0, w, tiles in groups:
                normalise(n, w)
                for k in range(first_turn[n], first_turn[n + 1]):
                    if k % 2 == 0:
                        take_probsT(dve, dve.tensor_copy, k)
                if n < 7:
                    maxima(n + 1, groups[n + 1][2], groups[n + 1][3])
                if n == 4:
                    dve.wait_ge(w_used, 4)
                for m in ((), (), (), (), (0, 1), (2, 3), (4, 5), (6,))[n]:
                    pool_block(m)
            dve.wait_ge(pT_ready, len(turns))
            dve.wait_ge(s_ready, 9)
            link(dve.memset(d_probs[:, :, 160:256], 0.0))
            link(tt(d_probs[:, :, 0:160], ps[:, 0:4, 0:160], cc("dec_mask", 4, 160), ALU.add))
            link(dve.tensor_reduce(d_stat[:, 0, :], d_probs[:, :, 0:160], AX_X, ALU.max, negate=True))
            link(ts(d_stat[:, 0, :], d_stat[:, 0, :], dec_sink[:, 1:2], None, ALU.min))
            ts(d_stat[:, 2, :], d_stat[:, 0, :], dec_sink[:, 0:1], None, ALU.add).then_inc(nmax_ready, 1)
            pool_block(7)
            dve.wait_ge(exp_ready, 9)
            link(tt(d_stat[:, 1, :], d_stat[:, 1, :], d_stat[:, 3, :], ALU.add))
            link(dve.reciprocal(d_stat[:, 1, :], d_stat[:, 1, :]))
            tt(d_probs[:, :, 0:160], d_probs[:, :, 0:160], over(d_stat[:, 1, :], 160), ALU.mult).then_inc(p_ready, 1)
            for g in range(0, 4, 2):
                take_probsT(dve, dve.tensor_copy, len(turns) + g)
            dve.wait_ge(nu_ready, 1)
            dve.tensor_copy(new_u[0:PAST_U, 0, :].rearrange("p (b n) -> p b n", b=2), ps[0:PAST_U, 0:2, :]).then_inc(nu_taken, 1)
            dve.tensor_copy(new_u[0:DEC, 1, :].rearrange("p (b n) -> p b n", b=2), ps[0:DEC, 2:4, :]).then_inc(nu_taken, 1)

            def merge(m, q, h):
                dve.wait_ge(sig_ready, q + 1)
                dve.wait_ge(branch_ready, q + 1)
                for j in range(2):
                    tt(gated[h][j], gates[h][j], ps[:, 4 * h + 2 + j, 0:HALF], ALU.mult).then_inc(gated_own, 1)
                dve.wait_ge(gated_own, q * 2 + 2)
                out = mergedT[:, bass.ds(m, 1), h * HALF:(h + 1) * HALF].squeeze(1)
                tt(out, gated[h][0], gated[h][1], ALU.add).then_inc(merged_ready, 1)

            with dve.Fori(0, KD) as m:
                for h in range(2):
                    merge(m, m * 2 + h, h)

            def take_hnT(t):
                dve.wait_ge(hnT_ready, t + 1)
                above(dve, logit_ready, t - 1)
                r = ROWS[t]
                dve.tensor_copy(hnT[t % 2][:, 0:4, 0:r], split(ps[:, 4, :], (4, P))[:, :, 0:r])\
                   .then_inc(hnT_taken[0], 1)

            dve.wait_ge(gffn_in, 16)
            for t in range(NT):
                r, bank = ROWS[t], 2 * (t % 2)
                dve.wait_ge(out_ready, t + 1)
                xr = x[0:r, t, :]
                if t < NT - 1:
                    ins = tt(split(xr, (2, 512)), ps[0:r, bank:bank + 2, :], split(xr, (2, 512)), ALU.add)
                else:
                    for q, cols in enumerate(slice(c, c + D // 4) for c in range(0, D, D // 4)):
                        ins = tt(xr[:, cols], ps[DEC * q:DEC * (q + 1), bank, 0:D // 4], xr[:, cols], ALU.add)
                ins.then_inc(x2_ready, 1)
                dve.wait_ge(root2_ready, t + 1)
                link(dve.reciprocal(stat[0:r, 2, t:t + 1], stat[0:r, 1, t:t + 1]))
                stt(hn[0:r, t, 0:D], xr, stat[0:r, 2, t:t + 1], g_ffn[0:r, :], ALU.mult, ALU.mult).then_inc(hn_ready, 1)
                if t:
                    take_hnT(t - 1)
            take_hnT(NT - 1)

            dve.wait_ge(logit_ready, NT)
            dve.wait_ge(y_start[0], 32)
            rows4 = NT - 1
            link(dve.memset(logits[:, NT - 1, :], 0.0))
            tt(logits[:, 0:rows4, :], split(ps[:, 6, 0:NT * 36], (NT, 36))[:, 0:rows4, :], across(r_bias[:], rows4), ALU.add)
            link(tt(logits[0:DEC, rows4, :], split(ps[:, 6, 0:NT * 36], (NT, 36))[0:DEC, rows4, :], r_bias[0:DEC, :], ALU.add))
            gl, el = logits[:, :, 0:NG], logits[:, :, NG:]
            g_max, g_share, e_max1, e_max2, w_first, w_second = vec

            def first_hot(hot, values, best, rank, tmp, n):
                link(tt(tmp, values, over(best, n), ALU.is_equal))
                link(tt(tmp, tmp, across(rank, NT), ALU.mult))
                link(dve.tensor_reduce(w_second, tmp, AX_X, ALU.max))
                link(tt(hot, tmp, over(w_second, n), ALU.is_equal))

            link(dve.tensor_reduce(g_max, gl, AX_X, ALU.max))
            tt(g_diff, gl, over(g_max, NG), ALU.subtract).then_inc(diff_ready, 1)
            first_hot(g_hot, gl, g_max, cc("group_rank"), g_tmp, NG)
            for g in range(NG):
                ins = tt(wide[:, :, g * EG:(g + 1) * EG], el[:, :, g * EG:(g + 1) * EG],
                         g_hot[:, :, g:g + 1].to_broadcast((P, NT, EG)), ALU.mult)
            link(ins)
            link(dve.tensor_reduce(picked, wide.rearrange("p t (g e) -> p t e g", g=NG), AX_X, ALU.add))
            link(dve.tensor_reduce(e_max1, picked, AX_X, ALU.max))
            first_hot(e_hot1, picked, e_max1, cc("expert_rank"), e_tmp, EG)
            link(stt(picked, e_hot1, -3.0e38, picked, ALU.mult, ALU.add))
            link(dve.tensor_reduce(e_max2, picked, AX_X, ALU.max))
            tt(e_diff, e_max2, e_max1, ALU.subtract).then_inc(diff_ready, 1)
            first_hot(e_hot2, picked, e_max2, cc("expert_rank"), e_tmp, EG)
            for g in range(NG):
                cols = slice(g * EG, (g + 1) * EG)
                tt(hot1[:, :, cols], e_hot1, g_hot[:, :, g:g + 1].to_broadcast((P, NT, EG)), ALU.mult)
                ins = tt(hot2[:, :, cols], e_hot2, g_hot[:, :, g:g + 1].to_broadcast((P, NT, EG)), ALU.mult)
            link(ins)
            link(tt(wide, hot1, hot2, ALU.add))
            tt(one_hot_bf[:], wide, over(cc("live"), NE), ALU.mult).then_inc(choice_ready, 1)
            dve.wait_ge(choice_ready, 1)
            for c, hot in ((0, hot1), (1, hot2)):
                link(tt(wide, hot, across(cc("expert_id"), NT), ALU.mult))
                link(dve.tensor_reduce(hn[:, :, D + 1 + 2 * c:D + 2 + 2 * c], wide, AX_X, ALU.add))
            dve.wait_ge(gexp_ready, 2)
            link(dve.tensor_reduce(g_share, g_exp, AX_X, ALU.add))
            link(dve.reciprocal(g_share, g_share))
            link(ts(w_second, e_exp, 1.0, None, ALU.add))
            link(dve.reciprocal(w_second, w_second))
            link(tt(w_first, g_share, w_second, ALU.mult))
            link(tt(w_second, w_first, e_exp, ALU.mult))
            dve.tensor_copy(hn[:, :, D + 2:D + 3], w_first.unsqueeze(2))
            dve.tensor_copy(hn[:, :, D + 4:D + 5], w_second.unsqueeze(2))
            dve.memset(hn[:, :, D + 5:XW], 0.0)
            for t in range(NT):
                ts(hn[:, t, D:D + 1], cc("row"), float(t * P), None, ALU.add)

            def exclusive_sum(out, v, cum):
                link(dve.memset(cum[0][:, 0:NE], 0.0))
                link(dve.memset(cum[1][:, 0:NE], 0.0))
                link(dve.tensor_copy(cum[0][:, NE:], v))
                n, s = 1, 0
                while n < NE:
                    link(tt(cum[1 - s][:, NE:], cum[s][:, NE:], cum[s][:, NE - n:2 * NE - n], ALU.add))
                    n, s = 2 * n, 1 - s
                link(tt(out, cum[s][:, NE:], v, ALU.subtract))

            dve.wait_ge(count_ready, 1)
            link(dve.tensor_copy(count[:], ps[:, 7, 256:256 + NE]))
            exclusive_sum(start[:], count[:], cum)
            link(dve.tensor_copy(start_i[:], start[:]))
            link(tt(wide, split(ps[:, 7, 0:NT * NE], (NT, NE)), across(start[:], NT), ALU.add))
            link(tt(hot1, hot1, wide, ALU.mult))
            link(tt(hot2, hot2, wide, ALU.mult))
            link(dve.tensor_reduce(vec[0], hot1, AX_X, ALU.add))
            link(dve.tensor_reduce(vec[1], hot2, AX_X, ALU.add))
            dve.tensor_copy(place_i[:, :, 0:1], vec[0].unsqueeze(2))
            dve.tensor_copy(place_i[:, :, 1:2], vec[1].unsqueeze(2)).then_inc(place_ready, 1)

            def row_chain(n):
                dve.wait_ge(row_own, n)

            def take_x(e, s, full):
                dve.wait_ge(xr_full[s], full)
                dve.tensor_copy(row_meta[s][0:C, :], x_rows[s][0:C, D:D + 5]).then_inc(row_own, 1)
                dve.wait_ge(xe_ready, e + 1)
                dve.tensor_copy(xT[s], split(ps[:, s, :], (JX, C))).then_inc(xe_taken, 1)

            N_ROW = 6

            def weights(e, s, expert):
                m, t = row_meta[s][0:C, :], row_tmp[0:C, :]
                row_chain(e * N_ROW + 1)
                ts(t[:, 0:1], m[:, 1:2], expert, m[:, 2:3], ALU.is_equal, ALU.mult).then_inc(row_own, 1)
                ts(t[:, 1:2], m[:, 3:4], expert, m[:, 4:5], ALU.is_equal, ALU.mult).then_inc(row_own, 1)
                row_chain(e * N_ROW + 3)
                tt(row_w[s][0:C, :], t[:, 0:1], t[:, 1:2], ALU.add).then_inc(row_own, 1)
                row_chain(e * N_ROW + 4)

            def hidden(e, s):
                dve.wait_ge(silu_ready, e + 1)
                stt(hid[s][0:C, :], ps[0:C, 2 + s, :], row_w[s][0:C, :], silu[s][0:C, :], ALU.mult, ALU.mult)\
                    .then_inc(hid_ready, 1)

            def targets(e, s, left, before):
                m, t = row_meta[s][0:C, :], row_tmp[0:C, :]
                ts(t[:, 2:3], cc("row")[0:C, :], left, None, ALU.is_lt).then_inc(row_own, 1)
                tt(t[:, 3:4], m[:, 0:1], cc("spare")[0:C, :], ALU.subtract).then_inc(row_own, 1)
                row_chain(e * N_ROW + 6)
                above(dve, y_out[s], y_written(s, before))
                stt(row_i[s][0:C, :], t[:, 3:4], t[:, 2:3], cc("spare")[0:C, :], ALU.mult, ALU.add)\
                    .then_inc(row_i_ready, 1)

            def take_y(e, s, before):
                dve.wait_ge(dn_ready, e + 1)
                above(dve, y_out[s], y_written(s, before))
                dve.tensor_copy(y_rows[s][0:C, 0:512], ps[0:C, 6 + s, :]).then_inc(y_taken[0], 1)

            def column(table, e):
                return table[0:C, e:e + 1] if isinstance(e, int) else table[0:C, bass.ds(e, 1)]

            def step(e, k, half, last=False):
                s = k % 2
                weights(e, s, column(cc("expert_id"), e))
                hidden(e, s)
                targets(e, s, column(count[:], e), half)
                if not last:
                    take_x(e + 1, 1 - s, (half + 1 + s) * 16)

                if not isinstance(e, int) or e > 0:
                    take_y(e - 1, 1 - s, half - (1 - s))

            def list_items():
                at = [OV]

                def take(*shape):
                    n = int(np.prod(shape))
                    at[0] += n
                    return area(at[0] - n, *shape)

                more, before, base, left0 = (take(NE) for _ in range(4))
                edges = take(NE, 8)
                cums = [take(2 * NE) for _ in range(2)]
                sel, tmp = take(NOV, NE), take(NOV, NE)
                steps, total = take(NOV), take(1)
                link(tt(edges, over(count[:], 8), across(cc("chunk_edge"), NE), ALU.is_gt))
                link(dve.tensor_reduce(more, edges, AX_X, ALU.add))
                exclusive_sum(before, more, cums)
                link(stt(base, before, -float(C), start[:], ALU.mult, ALU.add))
                link(ts(base, base, float(C), None, ALU.add))
                link(stt(left0, before, float(C), count[:], ALU.mult, ALU.add))
                link(ts(left0, left0, -float(C), None, ALU.add))
                link(tt(sel, over(cc("item"), NE), across(before, NOV), ALU.is_ge))
                link(tt(before, before, more, ALU.add))
                link(tt(tmp, over(cc("item"), NE), across(before, NOV), ALU.is_lt))
                link(tt(sel, sel, tmp, ALU.mult))
                for c, v in enumerate((cc("expert_id"), base, left0)):
                    link(tt(tmp, sel, across(v, NOV), ALU.mult))
                    link(dve.tensor_reduce(item[:, c, :], tmp, AX_X, ALU.add))
                link(ts(steps, cc("item"), float(C), None, ALU.mult))
                link(tt(item[:, 1, :], item[:, 1, :], steps, ALU.add))
                link(tt(item[:, 2, :], item[:, 2, :], steps, ALU.subtract))
                link(dve.tensor_copy(item_i[:], item[:, 0:2, :]))
                link(dve.tensor_reduce(total, more, AX_X, ALU.add))
                dve.tensor_copy(n_item_i[:], total).then_inc(item_ready, 1)

            take_x(0, 0, 16)
            dve.wait_ge(y_start[0], 32)
            dve.wait_ge(y_start[1], 16 * (NT - 2))
            step(0, 0, 0)
            list_items()
            for k in range(1, 1 + UNROLL):
                step(k, k, k // 2)
            with dve.Fori(1, STEPS) as it:
                for k in range(1, 1 + UNROLL):
                    step(it * UNROLL + k, k, it * (UNROLL // 2) + k // 2)
            step(NE - 1, 1, (NE - 1) // 2, last=True)
            take_y(NE - 1, 1, NE // 2 - 1)
            dve.wait_ge(item_ready, 1)
            n_item = dve.value_load(n_item_i[0:1, 0:1], min_val=0, max_val=NOV)
            with dve.If(n_item > 0):
                with dve.Fori(0, n_item) as i:
                    take_x(i + NE, 0, i * 16 + 16 * (NE // 2 + 1))
                    weights(i + NE, 0, item[0:C, 0, bass.ds(i, 1)])
                    hidden(i + NE, 0)
                    targets(i + NE, 0, item[0:C, 2, bass.ds(i, 1)], i + NE // 2)
                    take_y(i + NE, 0, i + NE // 2)

        @block.tensor
        def _(pe):
            mm, transpose = pe.matmul, pe.transpose

            pe.wait_ge(ident_in, 32)
            for t in range(NT):
                r = ROWS[t]
                pe.wait_ge(xs_ready, t + 1)
                above(pe, hT_ready, t - 1)
                for k in range(KD):
                    ins = transpose(ps[:, 2 * (t % 2) + k // 4, (k % 4) * P:(k % 4) * P + r],
                                    xs[t % 2][0:r, k * P:(k + 1) * P], ident[0:r, 0:r])
                ins.then_inc(xsT_ready, 1)

            def rotT(n):
                u, t = n // NT, n % NT
                r = ROWS[t]
                pe.wait_ge(rot_ready, n + 1)
                above(pe, rotT_taken, n - 1)
                if n < 2:
                    pe.wait_ge(hT_ready, NT)
                if u == 0:
                    transpose(ps[:, n % 2, 0:r], k_rows[0:r, t, :], ident[0:r, 0:r]).then_inc(rotT_ready, 1)
                    return
                for i in range(4):
                    ins = transpose(ps[:, n % 2, i * P:i * P + r], q_rows[n % 2][0:r, i * P:(i + 1) * P], ident[0:r, 0:r])
                ins.then_inc(rotT_ready, 1)

            def quarters_product(bank, tokens, w, n):
                for k in range(KD):
                    for q in range(4):
                        ins = mm(ps[DEC * q:DEC * (q + 1), bank, 0:n], tokens[:, k, SEQ:], w[:, k, q * n:(q + 1) * n],
                                 start=k == 0, stop=k == KD - 1)
                return ins

            for n in range(3 * NT):
                u, t = n // NT, n % NT
                r, w, bank = ROWS[t], (256 if u == 0 else 512), 4 + n % 4
                if t == 0:
                    pe.wait_ge(w_full[u % 2], (16, 32, 48)[u])
                if u == 0:
                    pe.wait_ge(hT_ready, t + 1)
                above(pe, z_taken, n - 3)
                if t == NT - 1 and u > 0:
                    ins = quarters_product(bank, hT, slot(u, KD, w), w // 4)
                else:
                    for k in range(KD):
                        ins = mm(ps[0:r, bank, 0:w], hT[:, k, t * P:t * P + r], slot(u, KD, w)[:, k, :],
                                 start=k == 0, stop=k == KD - 1)
                ins.then_inc(z_ready, 1)
                if n:
                    rotT(n - 1)
                if t == NT - 1:
                    pe.wait_ge(z_ready, n + 1)
                    pe.sem_inc(w_used, 1)
            rotT(3 * NT - 1)

            pe.wait_ge(state_in, 16)
            for m in range(KD):
                ins = transpose(ps[:, 2 + m // 4, (m % 4) * P:(m % 4) * P + DEC_B * PAST_U],
                                past_u[0:DEC_B * PAST_U, m * P:(m + 1) * P], ident[0:DEC_B * PAST_U, 0:DEC_B * PAST_U])
            ins.then_inc(pastT_ready, 1)
            pe.wait_ge(cache_in, 32)
            pe.wait_ge(z_taken, 3 * NT)
            for b in range(DEC_B):
                ins = transpose(ps[:, 4 + b // 4, (b % 4) * P:(b % 4 + 1) * P], kc_rows[:, b, :], ident)
            ins.then_inc(kcT_ready, 1)

            def pool_input(m, h):
                n = 3 + m // 4
                if m % 4 == 0 and h == 0:
                    pe.wait_ge(w_full[n % 2], (48, 64)[m // 4])
                above(pe, u_taken, 2 * m + h)
                for k in range(KD):
                    ins = mm(ps[:, 7, 0:HALF], slot(n, KD, 512)[:, k, (m % 4) * P:(m % 4 + 1) * P],
                             hT[:, k, h * HALF:(h + 1) * HALF], start=k == 0, stop=k == KD - 1)
                ins.then_inc(u_ready, 1)
                if m % 4 == 3 and h == 1:
                    pe.wait_ge(u_ready, 2 * m + 2)
                    pe.sem_inc(w_used, 1)

            def mix(m):
                g, c = m // 2, m % 2
                pe.wait_ge(pooled_ready, 2 * g + 2)
                above(pe, mix_taken, m - 1)
                for h in range(2):
                    for k in range(2):
                        ins = mm(ps[:, 4 + 2 * c + h, 0:HALF], slot(5, KD, 256)[:, 2 * g + k, c * P:(c + 1) * P],
                                 pooledT[:, 2 * g + k, h * HALF:(h + 1) * HALF], start=k == 0, stop=k == 1)
                ins.then_inc(mix_ready, 1)

            groups = list(head_groups())

            def scores(n):
                _, b, i0, w, tiles = groups[n]
                if n == 0:
                    pe.wait_ge(rotT_taken, 3 * NT)
                    pe.wait_ge(pastT_taken, 1)
                above(pe, exp_ready, n)
                for i in range(4):
                    out = ps[:, i, 0:2 * w].rearrange("p (v k) -> p v k", v=NKV)
                    mm(out, qT[:, i0 + i, b * P:(b + 1) * P], kT_pad[:, :, tiles[0] * P:(b + 1) * P],
                       start=True, stop=False)
                    ins = mm(out, ident_bf, band[:, :, 2 * P - w:], start=False, stop=True)
                ins.then_inc(s_ready, 1)

            def probsT_turn(n, k, kb, v, w):
                above(pe, pT_taken[k % 2], k // 2)
                pb = split(probs[n % 2][:, 0:8 * w], (4, NKV, w))
                for i in range(4):
                    ins = transpose(ps[:, 4 + k % 2, i * P:(i + 1) * P], pb[:, i, v, kb * P:(kb + 1) * P], ident)
                ins.then_inc(pT_ready, 1)

            def decoded_scores():
                pe.wait_ge(exp_ready, 8)
                for g in range(4):
                    for bb in range(2):
                        for v in range(NKV):
                            b, p = 2 * g + bb, 32 * (2 * bb + v)
                            q = q_decT[:, b, :, :].rearrange("p i s -> p (i s)")
                            mm(ps[p:p + 32, g, 0:P], q, kcT_pad[:, b, v, :], start=True, stop=True)
                            ins = mm(ps[p:p + 32, g, P:P + DEC], q, kT_pad[:, v, SEQ:], start=True, stop=True)
                ins.then_inc(s_ready, 1)

            scores(0)
            pe.wait_ge(kcT_taken, 1)
            for n, b, i0, w, tiles in groups:
                pool_input(n, 0)
                if n < 7:
                    scores(n + 1)
                else:
                    decoded_scores()
                pe.wait_ge(p_ready, n + 1)
                mine = range(first_turn[n], first_turn[n + 1])
                for k in mine:
                    probsT_turn(n, k, turns[k][1], turns[k][2], w)
                pool_input(n, 1)
                above(pe, o_taken, n)
                for k in mine:
                    _, kb, v = turns[k]
                    pe.wait_ge(pT_taken[k % 2], k // 2 + 1)
                    ins = mm(ps[64 * v:64 * v + 64, 6, :], v_rows[:, tiles[kb], 64 * v:64 * v + 64], probsT[k % 4],
                             start=kb == 0, stop=kb == len(tiles) - 1)
                ins.then_inc(o_ready, 1)
            pe.wait_ge(w_full[1], 64)
            pe.wait_ge(o_taken, 8)
            pe.wait_ge(u_taken, 2 * KD)
            for m in range(MIX_EARLY):
                mix(m)
            pe.wait_ge(p_ready, 9)
            for g in range(4):
                k = len(turns) + g
                if g == 0:
                    pe.wait_ge(mix_taken, 1)
                pe.wait_ge(pT_taken[k % 2], k // 2)
                for c in range(2):
                    ins = transpose(ps[:, 4 + k % 2, c * P:(c + 1) * P], d_probs[:, g, c * P:(c + 1) * P], ident)
                ins.then_inc(pT_ready, 1)
                pe.wait_ge(pT_taken[k % 2], k // 2 + 1)
                if g < 2:
                    pe.wait_ge(mix_taken, MIX_EARLY)
                else:
                    pe.wait_ge(o_taken, 7 + g)
                for bb in range(2):
                    for v in range(NKV):
                        b, rows, cols = 2 * g + bb, slice(64 * v, 64 * v + 64), slice(32 * bb, 32 * bb + 32)
                        at = 32 * (2 * bb + v)
                        mm(ps[rows, 6 + g % 2, cols], vc_rows[:, b, rows], probsT[k % 4][:, at:at + 32],
                           start=True, stop=False)
                        ins = mm(ps[rows, 6 + g % 2, cols], v_rows[:, 4, rows], probsT[k % 4][:, P + at:P + at + 32],
                                 start=False, stop=True)
                ins.then_inc(o_ready, 1)
            for m in range(KD):
                transpose(ps[0:PAST_U, m // 4, (m % 4) * P:(m % 4 + 1) * P],
                          uT[:, m, UP + SEQ - PAST_U:UP + SEQ], ident)
                ins = transpose(ps[0:DEC, 2 + m // 4, (m % 4) * P:(m % 4 + 1) * P],
                                u_decT[:, m, :], ident)
            ins.then_inc(nu_ready, 1)

            pe.wait_ge(pT_taken[0], len(turns) // 2 + 2)
            pe.wait_ge(pT_taken[1], len(turns) // 2 + 2)
            pe.wait_ge(o_taken, 12)
            for m in range(MIX_EARLY, KD):
                mix(m)
            pe.wait_ge(mix_ready, KD)
            pe.sem_inc(w_used, 1)
            pe.wait_ge(mix_taken, KD)
            pe.wait_ge(nu_taken, 2)

            def merge(q, h, s):
                w = area(w_slot[s], 4, KD, P)
                for j, src in enumerate((hT, hT, attnT, mixedT)):
                    for k in range(KD):
                        ins = mm(ps[:, 4 * h + j, 0:HALF], w[:, j, k, :], src[:, k, h * HALF:(h + 1) * HALF],
                                 start=k == 0, stop=k == KD - 1)
                    if j == 1:
                        ins.then_inc(gates_ready, 1)
                ins.then_inc(branch_ready, 1)

            for s in range(2):
                pe.wait_ge(w_full[s], 64 + 80)
                for h in range(2):
                    above(pe, merged_ready, 2 * s + h - 1)
                    merge(2 * s + h, h, s)
            with pe.Fori(1, KD // 2) as it:
                for s in range(2):
                    pe.wait_ge(w_full[s], it * 80 + (64 + 80))
                    for h in range(2):
                        pe.wait_ge(merged_ready, it * 4 + (2 * s + h - 1))
                        merge(it * 4 + (2 * s + h), h, s)

            def rows_out(t):
                r, bank = ROWS[t], 2 * (t % 2)
                above(pe, x2_ready, t - 1)
                if t == NT - 1:
                    ins = quarters_product(bank, mergedT, w_out, D // 4)
                    ins.then_inc(out_ready, 1)
                    return
                for c in range(2):
                    for k in range(KD):
                        ins = mm(ps[0:r, bank + c, :], mergedT[:, k, t * P:t * P + r], w_out[:, k, c * 512:(c + 1) * 512],
                                 start=k == 0, stop=k == KD - 1)
                ins.then_inc(out_ready, 1)

            def rows_T(t):
                r = ROWS[t]
                pe.wait_ge(hn_ready, t + 1)
                for s in range(2):
                    above(pe, hnT_taken[s], t)
                for k in range(KD):
                    ins = transpose(ps[:, 4 + k // 4, (k % 4) * P:(k % 4) * P + r], hn[0:r, t, k * P:(k + 1) * P],
                                    ident[0:r, 0:r])
                ins.then_inc(hnT_ready, 1)

            def route(t):
                r = ROWS[t]
                for s in range(2):
                    pe.wait_ge(hnT_taken[s], t + 1)
                for k in range(KD):
                    ins = mm(ps[0:r, 6, t * 36:(t + 1) * 36], hnT[t % 2][:, k, 0:r], w_route[:, k, :],
                             start=k == 0, stop=k == KD - 1)
                ins.then_inc(logit_ready, 1)

            pe.wait_ge(wo_in, 32)
            pe.wait_ge(route_in, 32)
            pe.wait_ge(merged_ready, 2 * KD)
            for t in range(NT + 1):
                if t < NT:
                    rows_out(t)
                if t > 1:
                    route(t - 2)
                if t > 0:
                    rows_T(t - 1)
            route(NT - 1)
            pe.wait_ge(choice_ready, 1)
            for t in range(NT):
                for j in range(t + 1):
                    mm(ps[:, 7, t * NE:(t + 1) * NE], before_bf if j == t else ones_bf, one_hot_bf[:, j, :],
                       start=j == 0, stop=j == t)
            for t in range(NT):
                ins = mm(ps[:, 7, 256:256 + NE], ones_bf, one_hot_bf[:, t, :], start=t == 0, stop=t == NT - 1)
            ins.then_inc(count_ready, 1)

            def before_transposing(sem, value):
                pe.wait_ge(sem, value)
                pe.sem_inc(passed_pe, 1)

            def turn_x(e, s, full):
                before_transposing(xr_full[s], full)
                rows = x_rows[s][0:C, 0:D].rearrange("c (p j) -> c j p", j=JX)
                for j in range(JX):
                    ins = transpose(ps[:, s, j * C:(j + 1) * C], rows[:, j, :], ident[0:C, 0:C])
                ins.then_inc(xe_ready, 1)

            def gate_up(e, s, ring, full):
                pe.wait_ge(xe_taken, e + 1)
                pe.wait_ge(gu_full[ring], full)
                for j in range(JX):
                    mm(ps[0:C, 2 + s, :], xT[s][:, j, :], w_up[ring][:, j, :], start=j == 0, stop=j == JX - 1)
                    ins = mm(ps[64:64 + C, 2 + s, :], xT[s][:, j, :], w_gate[ring][:, j, :], start=j == 0, stop=j == JX - 1)
                ins.then_inc(gu_ready, 1)

            def turn_hid(e, s):
                before_transposing(hid_ready, e + 1)
                rows = hid[s][0:C, :].rearrange("c (p j) -> c j p", j=JH)
                for j in range(JH):
                    ins = transpose(ps[:, 4 + s, j * C:(j + 1) * C], rows[:, j, :], ident[0:C, 0:C])
                ins.then_inc(hidT_ready, 1)

            def down(e, s, ring, full):
                pe.wait_ge(hidT_taken, e + 1)
                pe.wait_ge(dn_full[ring], full)
                for q in range(2):
                    above(pe, y_taken[q], e - 1)
                for j in range(JH):
                    for q in range(2):
                        ins = mm(ps[64 * q:64 * q + C, 6 + s, :], hidT[s][:, j, :], w_down[ring][:, j, 512 * q:512 * q + 512],
                                 start=j == 0, stop=j == JH - 1)
                ins.then_inc(dn_ready, 1)

            def step(e, k, half, turn, last=False):
                s = k % 2
                if not last:
                    turn_x(e + 1, 1 - s, (half + 1 + s) * 16)
                ring, before = k % NSLOT, (k - 1) % NSLOT
                if not isinstance(e, int) or e > 0:
                    turn_hid(e - 1, 1 - s)
                gate_up(e, s, ring, (turn + 1) * 32)
                if not isinstance(e, int) or e > 0:
                    down(e - 1, 1 - s, before, (turn + 1 - (1 if ring == 0 else 0)) * 16)

            turn_x(0, 0, 16)
            step(0, 0, 0, 0)
            for k in range(1, 1 + UNROLL):
                step(k, k, k // 2, k // NSLOT)
            with pe.Fori(1, STEPS) as it:
                for k in range(1, 1 + UNROLL):
                    step(it * UNROLL + k, k, it * (UNROLL // 2) + k // 2, it * (UNROLL // NSLOT) + k // NSLOT)
            e = NE - 1
            step(e, e, e // 2, e // NSLOT, last=True)
            turn_hid(e, 1)
            down(e, 1, e % NSLOT, 16 * (e // NSLOT + 1))
            filled = -(-NE // NSLOT)
            pe.wait_ge(item_ready, 1)
            n_item = pe.value_load(n_item_i[0:1, 0:1], min_val=0, max_val=NOV)
            with pe.If(n_item > 0):
                with pe.Fori(0, n_item) as i:
                    turn_x(i + NE, 0, i * 16 + 16 * (NE // 2 + 1))
                    gate_up(i + NE, 0, 0, i * 32 + 32 * (filled + 1))
                    turn_hid(i + NE, 0)
                    down(i + NE, 0, 0, i * 16 + 16 * (filled + 1))


def kernel(x_prompt, x_sample, cache_k, cache_v, state_pool, norm_mix_g, w_in, q_norm_g, k_norm_g, attn_sinks,
           w_attn_branch, pool_mix_w, pool_scale, w_pool_branch, w_out, norm_ffn_g, w_route_group,
           b_route_group, w_route_expert, b_route_expert, w_expert_gate, w_expert_up, w_expert_down):
    import concourse.bacc as bacc
    from concourse.bass_utils import run_bass_kernel_spmd

    f = np.asarray
    arrays = {
        "x": np.concatenate([f(x_prompt).reshape(SEQ, D), f(x_sample).reshape(DEC, D)]),
        "cache_k": f(cache_k).reshape(DEC_B, WIN, P), "cache_v": f(cache_v).reshape(DEC_B, WIN, P),
        "state": f(state_pool).reshape(DEC_B, PAST_U, D),
        "g_mix": f(norm_mix_g).reshape(KD, P).T, "w_in": f(w_in)[0], "gq": f(q_norm_g)[0], "gk": f(k_norm_g)[0],
        "sinks": f(attn_sinks)[0],
        "dec_sinks": np.tile(np.repeat(f(attn_sinks)[0], DEC_S), 2).reshape(P, 1),
        "w_attn": f(w_attn_branch)[0], "w_mix": f(pool_mix_w).reshape(D, 256), "p_scale": f(pool_scale).reshape(KD, P).T,
        "w_pool": f(w_pool_branch)[0], "w_out": f(w_out)[0], "g_ffn": f(norm_ffn_g)[0],
        "w_group": f(w_route_group)[0], "b_group": f(b_route_group)[0],
        "w_expert": f(w_route_expert)[0], "b_expert": f(b_route_expert)[0],
        "w_eg": f(w_expert_gate)[0], "w_eu": f(w_expert_up)[0], "w_ed": f(w_expert_down)[0],
        "const": constants(),
    }
    outs = {"y": (T + C, D), "kp": (WIN, P), "vp": (WIN, P), "up": (PAST_U, D),
            "ks": (DEC_B, WIN, P), "vs": (DEC_B, WIN, P), "us": (DEC_B, PAST_U, D)}
    nc = bacc.Bacc("TRN2", target_bir_lowering=False, num_devices=1)
    a, o = {}, {}
    for name, v in arrays.items():
        arrays[name] = v = np.ascontiguousarray(v)
        a[name] = nc.dram_tensor(f"in_{name}", v.shape, mybir.dt.from_np(v.dtype), kind="ExternalInput").ap()
    for name, shape in outs.items():
        o[name] = nc.dram_tensor(f"out_{name}", shape, F32, kind="ExternalOutput").ap()
    a["w_eg"] = a["w_eg"].rearrange("e (p j) n -> e p j n", j=JX)
    a["w_eu"] = a["w_eu"].rearrange("e (p j) n -> e p j n", j=JX)
    a["w_ed"] = a["w_ed"].rearrange("e (p j) n -> e p j n", j=JH)
    build(nc, a, o)
    r = run_bass_kernel_spmd(nc, [{f"in_{n}": v for n, v in arrays.items()}], core_ids=[0]).results[0]
    got = {n: r[f"out_{n}"] for n in outs}
    kv = (1, -1, WIN, NKV, HD)
    return (got["y"][:SEQ].reshape(1, SEQ, D), got["y"][SEQ:T].reshape(DEC_B, DEC_S, D),
            got["kp"].reshape(kv), got["vp"].reshape(kv), got["up"].reshape(1, 1, PAST_U, D),
            got["ks"].reshape(kv), got["vs"].reshape(kv), got["us"].reshape(1, DEC_B, PAST_U, D))
```
